# Optimizing a Trainium2 kernel written in Bass

```python
import math
import jax, jax.numpy as jnp
from jax import lax
import numpy as np

D_MODEL = 1024
BATCH = 1
SEQ = 128
DEPTH = 2
DEC_BATCH = 1
DEC_SEQ = 512
PAST_LEN = 128

GRID_W = 64
D_CONV = 512
CONV_WIDTH = 31
N_HEADS = 4
HEAD_DIM = 64
V_DIM = 2 * HEAD_DIM
D_QK = N_HEADS * 2 * HEAD_DIM
D_ATTN = N_HEADS * V_DIM
D_MIX = D_CONV + D_ATTN
D_IN = 2 * D_CONV + 2 * D_QK + D_ATTN
N_EXPERTS = 16
EC_FACTOR = 2
D_EXPERT = 1024
ROPE_BASE = 10000.0
ROPE_AXIS = HEAD_DIM // 2
EPS = 1e-6
Q_BLOCK = 128

kernel_name = "hymba_conformer_diffattn_ec_dit_step"

def rms_norm(x, g):
    x32 = x.astype(jnp.float32)
    y = x32 * lax.rsqrt(jnp.mean(x32 * x32, axis=-1, keepdims=True) + EPS)
    return y.astype(x.dtype) * g

def modulation(cvec, w_mod, b_mod):
    m = jax.nn.silu(cvec) @ w_mod + b_mod
    return jnp.split(m, 6, axis=-1)

def axial_rope_tables(T):
    rows = T // GRID_W
    row = jnp.repeat(jnp.arange(rows, dtype=jnp.float32), GRID_W)
    col = jnp.tile(jnp.arange(GRID_W, dtype=jnp.float32), rows)
    inv = ROPE_BASE ** (-jnp.arange(0, ROPE_AXIS, 2, dtype=jnp.float32) / ROPE_AXIS)
    ar = row[:, None] * inv
    ac = col[:, None] * inv
    shp = (1, T, 1, 1, ROPE_AXIS // 2)
    return (jnp.cos(ar).reshape(shp), jnp.sin(ar).reshape(shp),
            jnp.cos(ac).reshape(shp), jnp.sin(ac).reshape(shp))

def rotate_half_pairs(x, cos, sin):
    n = x.shape[-1] // 2
    x1, x2 = x[..., :n], x[..., n:]
    cos = cos.astype(x.dtype)
    sin = sin.astype(x.dtype)
    return jnp.concatenate([x1 * cos - x2 * sin, x2 * cos + x1 * sin], axis=-1)

def apply_axial_rope(x, rope):
    cos_r, sin_r, cos_c, sin_c = rope
    return jnp.concatenate([rotate_half_pairs(x[..., :ROPE_AXIS], cos_r, sin_r),
                            rotate_half_pairs(x[..., ROPE_AXIS:], cos_c, sin_c)], axis=-1)

def diff_attention(q, k, v, lam):
    B, S = q.shape[0], q.shape[1]
    nb = S // Q_BLOCK
    qb = q.reshape(B, nb, Q_BLOCK, N_HEADS, 2, HEAD_DIM).transpose(1, 0, 2, 3, 4, 5)
    scale = HEAD_DIM ** -0.5

    def one_block(qi):
        s = jnp.einsum('bqhcd,bkhcd->bchqk', qi, k).astype(jnp.float32) * scale
        p = jax.nn.softmax(s, axis=-1)
        a = p[:, 0] - lam * p[:, 1]
        return jnp.einsum('bhqk,bkhv->bqhv', a.astype(v.dtype), v)

    o = lax.map(one_block, qb)
    return o.transpose(1, 0, 2, 3, 4).reshape(B, S, N_HEADS, V_DIM)

def conv_module(a, g, conv_w, conv_b, ln_g, ln_b):
    u = a * jax.nn.sigmoid(g)
    u = lax.conv_general_dilated(
        u, conv_w[:, None, :].astype(u.dtype), window_strides=(1,),
        padding=[(CONV_WIDTH // 2, CONV_WIDTH // 2)],
        dimension_numbers=('NWC', 'WIO', 'NWC'), feature_group_count=D_CONV) + conv_b
    u32 = u.astype(jnp.float32)
    mu = jnp.mean(u32, axis=-1, keepdims=True)
    var = jnp.mean((u32 - mu) ** 2, axis=-1, keepdims=True)
    un = ((u32 - mu) * lax.rsqrt(var + EPS)).astype(u.dtype) * ln_g + ln_b
    return jax.nn.silu(un)

def expert_choice(h, w_router, w_gate, w_up, w_down):
    B, T, D = h.shape
    C = EC_FACTOR * T // N_EXPERTS
    aff = jax.nn.softmax(jnp.einsum('btd,de->bte', h, w_router).astype(jnp.float32), axis=-1)
    gsel, idx = lax.top_k(aff.transpose(0, 2, 1), C)
    xs = jax.vmap(lambda hb, ib: hb[ib])(h, idx)
    hid = jax.nn.silu(jnp.einsum('becd,edf->becf', xs, w_gate)) * jnp.einsum('becd,edf->becf', xs, w_up)
    ye = jnp.einsum('becf,efd->becd', hid, w_down) * gsel[..., None].astype(h.dtype)
    return jax.vmap(lambda yb, ib: jnp.zeros((T, D), yb.dtype).at[ib.reshape(-1)].add(yb.reshape(-1, D)))(ye, idx)

def trunk_layer(x, cvec, layer_idx, rope, ctx_k, ctx_v, norm1_g, w_mod, b_mod, w_in, conv_w, conv_b,
                conv_ln_g, conv_ln_b, lambda_q1, lambda_k1, lambda_q2, lambda_k2, subln_g, w_out,
                norm2_g, w_router, w_gate, w_up, w_down):
    B, T, _ = x.shape
    sh1, sc1, g1, sh2, sc2, g2 = modulation(cvec, w_mod, b_mod)
    h = rms_norm(x, norm1_g) * (1 + sc1) + sh1
    z = h @ w_in
    conv_a, conv_g, q, k, v = jnp.split(
        z, [D_CONV, 2 * D_CONV, 2 * D_CONV + D_QK, 2 * D_CONV + 2 * D_QK], axis=-1)
    q = q.reshape(B, T, N_HEADS, 2, HEAD_DIM)
    k = k.reshape(B, T, N_HEADS, 2, HEAD_DIM)
    v = v.reshape(B, T, N_HEADS, V_DIM)
    if rope is None:
        keys, vals = k, v
    else:
        q = apply_axial_rope(q, rope)
        keys = jnp.concatenate([apply_axial_rope(k, rope), ctx_k.astype(k.dtype)], axis=1)
        vals = jnp.concatenate([v, ctx_v.astype(v.dtype)], axis=1)
    lam_init = 0.8 - 0.6 * math.exp(-0.3 * layer_idx)
    lam = (jnp.exp(jnp.sum(lambda_q1.astype(jnp.float32) * lambda_k1.astype(jnp.float32)))
           - jnp.exp(jnp.sum(lambda_q2.astype(jnp.float32) * lambda_k2.astype(jnp.float32))) + lam_init)
    o = diff_attention(q, keys, vals, lam)
    o = rms_norm(o, subln_g) * (1.0 - lam_init)
    mix = jnp.concatenate([conv_module(conv_a, conv_g, conv_w, conv_b, conv_ln_g, conv_ln_b),
                           o.reshape(B, T, D_ATTN)], axis=-1)
    x = x + g1 * (mix @ w_out)
    h2 = rms_norm(x, norm2_g) * (1 + sc2) + sh2
    x = x + g2 * expert_choice(h2, w_router, w_gate, w_up, w_down)
    return x, k, v

def setup_inputs(seed: int = 0) -> dict:
    key = jax.random.key(seed)
    ks = jax.random.split(key, 32)

    def nrm(k, shape, scale):
        return jax.random.normal(k, shape, jnp.float32) * scale

    gain = lambda k, shape: 1.0 + nrm(k, shape, 0.01)
    return {
        "x_prompt": nrm(ks[0], (BATCH, SEQ, D_MODEL), 1.0),
        "x_sample": nrm(ks[1], (DEC_BATCH, DEC_SEQ, D_MODEL), 1.0),
        "c": nrm(ks[2], (DEC_BATCH, D_MODEL), 1.0),
        "cache_k": nrm(ks[3], (DEC_BATCH, DEPTH, PAST_LEN, N_HEADS, 2, HEAD_DIM), 1.0),
        "cache_v": nrm(ks[4], (DEC_BATCH, DEPTH, PAST_LEN, N_HEADS, V_DIM), 1.0),
        "c_ctx": nrm(ks[5], (D_MODEL,), 1.0),
        "norm1_g": gain(ks[6], (DEPTH, D_MODEL)),
        "w_mod": nrm(ks[7], (DEPTH, D_MODEL, 6 * D_MODEL), 0.5 * D_MODEL ** -0.5),
        "b_mod": nrm(ks[8], (DEPTH, 6 * D_MODEL), 0.02),
        "w_in": nrm(ks[9], (DEPTH, D_MODEL, D_IN), D_MODEL ** -0.5),
        "conv_w": nrm(ks[10], (DEPTH, CONV_WIDTH, D_CONV), CONV_WIDTH ** -0.5),
        "conv_b": nrm(ks[11], (DEPTH, D_CONV), 0.02),
        "conv_ln_g": gain(ks[12], (DEPTH, D_CONV)),
        "conv_ln_b": nrm(ks[13], (DEPTH, D_CONV), 0.02),
        "lambda_q1": nrm(ks[14], (DEPTH, HEAD_DIM), 0.1),
        "lambda_k1": nrm(ks[15], (DEPTH, HEAD_DIM), 0.1),
        "lambda_q2": nrm(ks[16], (DEPTH, HEAD_DIM), 0.1),
        "lambda_k2": nrm(ks[17], (DEPTH, HEAD_DIM), 0.1),
        "subln_g": gain(ks[18], (DEPTH, V_DIM)),
        "w_out": nrm(ks[19], (DEPTH, D_MIX, D_MODEL), D_MIX ** -0.5),
        "norm2_g": gain(ks[20], (DEPTH, D_MODEL)),
        "w_router": nrm(ks[21], (DEPTH, D_MODEL, N_EXPERTS), D_MODEL ** -0.5),
        "w_gate": nrm(ks[22], (DEPTH, N_EXPERTS, D_MODEL, D_EXPERT), D_MODEL ** -0.5),
        "w_up": nrm(ks[23], (DEPTH, N_EXPERTS, D_MODEL, D_EXPERT), D_MODEL ** -0.5),
        "w_down": nrm(ks[24], (DEPTH, N_EXPERTS, D_EXPERT, D_MODEL), D_EXPERT ** -0.5),
        "final_norm_g": gain(ks[25], (D_MODEL,)),
    }

def reference(x_prompt, x_sample, c, cache_k, cache_v, c_ctx, norm1_g, w_mod, b_mod, w_in, conv_w,
              conv_b, conv_ln_g, conv_ln_b, lambda_q1, lambda_k1, lambda_q2, lambda_k2, subln_g,
              w_out, norm2_g, w_router, w_gate, w_up, w_down, final_norm_g):
    rope = axial_rope_tables(x_sample.shape[1])
    c_ctx_vec = c_ctx[None, None, :]
    c_lat = c[:, None, :]
    xp, xs = x_prompt, x_sample
    new_k, new_v = [], []
    for l in range(DEPTH):
        w = (norm1_g[l], w_mod[l], b_mod[l], w_in[l], conv_w[l], conv_b[l], conv_ln_g[l], conv_ln_b[l],
             lambda_q1[l], lambda_k1[l], lambda_q2[l], lambda_k2[l], subln_g[l], w_out[l], norm2_g[l],
             w_router[l], w_gate[l], w_up[l], w_down[l])
        xp, kp, vp = trunk_layer(xp, c_ctx_vec, l, None, None, None, *w)
        new_k.append(kp)
        new_v.append(vp)
        xs, _, _ = trunk_layer(xs, c_lat, l, rope, cache_k[:, l], cache_v[:, l], *w)
    y_prompt = rms_norm(xp, final_norm_g)
    y_sample = rms_norm(xs, final_norm_g)
    new_cache_k = jnp.stack(new_k, axis=1)
    new_cache_v = jnp.stack(new_v, axis=1)
    return (y_prompt, y_sample, new_cache_k, new_cache_v)


_drawn_inputs = setup_inputs


def setup_inputs(seed=0):
    import zlib

    import numpy as np

    out = dict(_drawn_inputs(seed))
    spreads = {}
    factors = {'norm1_g': 5.74,
     'conv_b': 6.766,
     'conv_ln_g': 8.0,
     'conv_ln_b': 8.0,
     'lambda_k2': 2.717,
     'subln_g': 8.0,
     'norm2_g': 6.4,
     'final_norm_g': 5.554}
    for name, (base, spread) in spreads.items():
        noise = np.random.default_rng([zlib.crc32(name.encode()), seed]).standard_normal(out[name].shape)
        drawn = base * np.exp(spread * noise) if base else spread * noise
        out[name] = __import__('jax').numpy.asarray(drawn.astype(out[name].dtype))
    for name, factor in factors.items():
        out[name] = (out[name] * factor).astype(out[name].dtype)
    return out
```

```python
import math
from contextlib import ExitStack

import numpy as np
import concourse.bass as bass
from concourse import mybir

D = 1024
DEPTH = 2
N_CTX, N_LAT, PAST = 128, 512, 128
N_TOK = N_CTX + N_LAT
H, HD = 4, 64
VD = 2 * HD
D_CONV, TAPS = 512, 31
GRID_W = 64
ROPE_BASE, ROPE_AXIS = 10000.0, HD // 2
EXPERTS, D_EXP = 16, 1024
CAP_CTX, CAP_LAT = 2 * N_CTX // EXPERTS, 2 * N_LAT // EXPERTS
CAP = CAP_LAT + CAP_CTX
EPS = 1e-6

P = 128
KD = D // P
TILES = N_TOK // P
CH = D_CONV // P
HALO = TAPS // 2
U_LEN = HALO + N_CTX + HALO + N_LAT + HALO
C_LEN = N_CTX + HALO + N_LAT
LAT0 = N_CTX + HALO
BANK = 512
UNIT = KD * BANK
SLOTS = 6
DENSE_SLOTS = 4
MOD_UNITS = 6 * D // BANK
PROJ_UNITS = (2 * D_CONV + 4 * H * HD + H * VD) // BANK
OUT_UNITS = 2
DENSE_UNITS = MOD_UNITS + PROJ_UNITS + OUT_UNITS
LAYER_UNITS = DENSE_UNITS + 6 * EXPERTS
MOD_FIRST = 4
D_PROJ = MOD_FIRST
D_MOD2 = D_PROJ + PROJ_UNITS
D_OUT = D_MOD2 + MOD_UNITS - MOD_FIRST
BLK = BANK // P
ATT = TILES * H
C_BMOD, C_N1, C_N2, C_CB, C_LG, C_LB, C_SUB, C_ALL = 0, 48, 56, 64, 68, 72, 76, 77


class Signal:

    def __init__(self, sem, per_layer, unit=1):
        self.sem, self.per_layer, self.unit = sem, per_layer, unit

    def at(self, layer, n):
        return self.sem, (n + layer * self.per_layer) * self.unit


def build(nc, x_prompt, x_sample, c, cache_k, cache_v, c_ctx, norm1_g, w_mod, b_mod, w_in, conv_w, conv_b,
          conv_ln_g, conv_ln_b, lambda_q1, lambda_k1, lambda_q2, lambda_k2, subln_g, w_out, norm2_g,
          w_router, w_gate, w_up, w_down, final_norm_g, rope_cos, rope_sin,
          y_prompt, y_sample, new_cache_k, new_cache_v):
    f32, u32 = mybir.dt.float32, mybir.dt.uint32
    ALU, ACT = mybir.AluOpType, mybir.ActivationFunctionType
    AX = mybir.AxisListType.X
    lam_init = [0.8 - 0.6 * math.exp(-0.3 * l) for l in range(DEPTH)]

    ctx = ExitStack()
    with ctx:
        def sb(name, shape, dt=f32):
            return ctx.enter_context(nc.sbuf_tensor(name, shape, dt))

        def signal(name, per_layer=0, unit=1):
            return Signal(ctx.enter_context(nc.semaphore(name)), per_layer, unit)

        x_res = nc.dram_tensor("x_res", (N_TOK, D), f32, kind="Internal").ap()
        x_unit = nc.dram_tensor("x_unit", (N_TOK, D), f32, kind="Internal").ap()

        ring = sb("weight_ring", [P, SLOTS, UNIT])
        free_slots = ring[:, DENSE_SLOTS:SLOTS, :].rearrange("p s n -> p (s n)")
        mix = sb("mix", [P, KD, N_TOK])
        u_gate = sb("u_gate", [P, CH * U_LEN])
        u = u_gate[:, :].rearrange("p (c n) -> p c n", c=CH)
        gate1 = u_gate[:, 0:2 * D].rearrange("p (v n) -> p v n", v=2)
        qk = sb("qk", [P, 2, H, N_TOK])
        q_t, k_t = qk[:, 0], qk[:, 1]
        qk_flat = qk[:, :, :, :].rearrange("p a h n -> p (a h n)")
        picked = qk_flat[0:CAP, 0:2 * D].rearrange("p (b n) -> p b n", b=2)
        added = qk_flat[0:CAP, 2 * D:4 * D].rearrange("p (b n) -> p b n", b=2)
        v_sb = sb("v_sb", [P, TILES * BANK])
        v_tok = v_sb[:, :].rearrange("p (t n) -> p t n", t=TILES)
        h2_t = v_sb[:, 0:D].rearrange("p (k n) -> p k n", k=KD)
        picked_t = v_sb[:, D:D + 2 * KD * CAP].rearrange("p (b k n) -> p b k n", b=2, k=KD)
        mix_flat = mix[:, :, :].rearrange("p k n -> p (k n)")
        hid = mix_flat[:, 0:KD * CAP].rearrange("p (k n) -> p k n", k=KD)
        silu_g = mix_flat[:, KD * CAP:2 * KD * CAP].rearrange("p (b n) -> p b n", b=2)
        x_tile = sb("x_tile", [P, 2, D])
        x_norm = sb("x_norm", [P, D])
        conv_tmp = sb("conv_tmp", [P, 2, C_LEN])
        key_rows = conv_tmp[:, 0, 0:BANK]
        acc = free_slots[:, 0:CH * C_LEN].rearrange("p (c n) -> p c n", c=CH)
        o = CH * C_LEN
        rope_tmp = free_slots[:, o:o + 2 * H * N_LAT].rearrange("p (b n) -> p b n", b=2 * H)
        prob = free_slots[:, o:o + 4 * N_TOK].rearrange("p (b c n) -> p b c n", b=2, c=2)
        a_row = free_slots[:, o + 4 * N_TOK:o + 6 * N_TOK].rearrange("p (b n) -> p b n", b=2)
        a_col = free_slots[:, o + 6 * N_TOK:o + 7 * N_TOK]
        conv_rstd = rope_tmp[:, 0:2, :].rearrange("p b n -> p (b n)")[:, 0:C_LEN]
        pool_tmp = free_slots[:, o + 2 * H * N_LAT:o + 2 * H * N_LAT + C_LEN]
        gate1_cols = free_slots[:, 0:2 * D].rearrange("p (v k n) -> p v k n", v=2, k=KD)
        gate2_cols = free_slots[:, 2 * D:2 * D + KD * CAP].rearrange("p (k n) -> p k n", k=KD)
        assert o + 2 * H * N_LAT + C_LEN <= 2 * UNIT
        o_tok = sb("o_tok", [P, 2, H, VD])
        o_sq = conv_tmp[:, 1, 0:BANK].rearrange("p (h n) -> p h n", h=H)
        q_pad = sb("q_pad", [P, 2, 2, P])
        map_scale = sb("map_scale", [P, 2])
        cos_sb = sb("cos_sb", [P, N_LAT])
        sin_sb = sb("sin_sb", [P, N_LAT])
        past_k_t = sb("past_k_t", [P, DEPTH, H, PAST])
        past_v = sb("past_v", [P, DEPTH, H * VD])
        gate2 = sb("gate2", [CAP, D])
        scale2_x = sb("scale2_x", [P, KD, CAP])
        shift2_x = sb("shift2_x", [P, KD, CAP])
        ident = sb("ident", [P, P])
        ones = sb("ones", [P, P])
        conv_cols = sb("conv_cols", [P, DEPTH, TAPS * CH])
        par_cols = sb("par_cols", [P, DEPTH, C_ALL])
        cond_rows = free_slots[0:2 * KD, 0:P]
        conv_rows = free_slots[0:TAPS * CH, P:P + DEPTH * P].rearrange("p (l n) -> p l n", l=DEPTH)
        par_rows = free_slots[0:C_ALL, 3 * P:3 * P + DEPTH * P].rearrange("p (l n) -> p l n", l=DEPTH)
        past_k = free_slots[:, 5 * P:5 * P + DEPTH * BANK].rearrange("p (l n) -> p l n", l=DEPTH)
        o = 5 * P + DEPTH * BANK
        lam_rows = free_slots[:, o:o + DEPTH * 4 * HD].rearrange("p (l f n) -> p l f n", l=DEPTH, f=4)
        o += DEPTH * 4 * HD
        lam_prod = free_slots[:, o:o + DEPTH * 2 * HD].rearrange("p (l f n) -> p l f n", l=DEPTH, f=2)
        cond_silu = sb("cond_silu", [P, 2, KD])
        lam_e = sb("lam_e", [P, DEPTH, 2])
        lam = sb("lam", [P, DEPTH])
        sub_cols = sb("sub_cols", [P, DEPTH])
        router = sb("router", [P, DEPTH, KD, EXPERTS])
        mod = sb("mod", [P, 6 * KD, 2])
        scale1 = sb("scale1", [P, KD, 2])
        scale2 = sb("scale2", [P, KD, 2])
        ssq = sb("ssq", [P, 3])
        mean_sq = sb("mean_sq", [P, 3])
        rstd = sb("rstd", [P, 3])
        neg_half = sb("neg_half", [P, H])
        eps = sb("eps", [P, 1])
        neg_max = sb("neg_max", [P, 2, 2, 2])
        neg_m = sb("neg_m", [P, 2, 2])
        row_sum = sb("row_sum", [P, 2, 2, 2])
        row_r = sb("row_r", [P, 2, 2])
        o_ss = sb("o_ss", [P, 2, H])
        o_rstd = sb("o_rstd", [P, 2, H])
        r_max = sb("r_max", [P, 1])
        r_sum = sb("r_sum", [P, 1])
        r_exp = sb("r_exp", [P, EXPERTS])
        aff = sb("aff", [P, EXPERTS])
        pick_space = qk_flat[0:EXPERTS, 4 * D:4 * D + N_TOK + 3 * CAP]
        aff_t = pick_space[:, 0:N_TOK]
        top_v = pick_space[:, N_TOK:N_TOK + CAP]
        top_f = pick_space[:, N_TOK + CAP:N_TOK + 2 * CAP]
        top_i = pick_space[:, N_TOK + 2 * CAP:N_TOK + 3 * CAP].bitcast(u32)
        row_idx = sb("row_idx", [CAP, EXPERTS], u32)
        gsel = sb("gsel", [CAP, EXPERTS])
        ps = ctx.enter_context(nc.psum_tensor("ps", [P, 8, BANK], f32))

        consts_ready = signal("consts_ready")
        cond_loaded = signal("cond_loaded", unit=16)
        rows_loaded = signal("rows_loaded", unit=16)
        misc_loaded = signal("misc_loaded", unit=16)
        residual_set = signal("residual_set", unit=16)
        setup_transposed = signal("setup_transposed")
        setup_copied = signal("setup_copied")
        cond_ready = signal("cond_ready")
        lam_summed = signal("lam_summed")
        lam_exped = signal("lam_exped")
        lam_ready = signal("lam_ready")
        slot_dense = [len(range(s, DENSE_UNITS, DENSE_SLOTS)) if s < DENSE_SLOTS else 0 for s in range(SLOTS)]
        slot_loaded = [signal(f"slot{s}_loaded", slot_dense[s] + EXPERTS, 16) for s in range(SLOTS)]
        unit_used = signal("unit_used", LAYER_UNITS)
        mod1_ready = signal("mod1_ready", 1)
        mod2_ready = signal("mod2_ready", 1)
        x_loaded = [signal(f"x_loaded{b}", 6 - 2 * b, 16) for b in range(2)]
        ssq_ready = signal("ssq_ready", TILES)
        mean_sq_ready = signal("mean_sq_ready", TILES)
        rstd_ready = signal("rstd_ready", TILES)
        x_norm_ready = signal("x_norm_ready", TILES)
        x_transposed = signal("x_transposed", TILES)
        h_lo_ready = signal("h_lo_ready", TILES)
        h_hi_ready = signal("h_hi_ready", TILES)
        halo_zero = signal("halo_zero", 1)
        proj_done = signal("proj_done", 4 * (BLK - 1) + TILES - 1)
        proj_copied = signal("proj_copied", 4 * BLK + TILES)
        glu_ready = signal("glu_ready", CH)
        rope_shuffled = signal("rope_shuffled", 2 * H)
        rope_ready = signal("rope_ready", 2 * H)
        conv_ready = signal("conv_ready", CH - 1)
        conv3_ready = signal("conv3_ready", 1)
        keys_transposed = signal("keys_transposed", 1)
        keys_copied = signal("keys_copied", 1)
        cache_stored = signal("cache_stored", 2, 16)
        mean_ready = signal("mean_ready", 1)
        centred = signal("centred", CH)
        squared = signal("squared", CH)
        square_used = signal("square_used", CH)
        conv_std_ready = signal("conv_std_ready", 1)
        conv_normed = signal("conv_normed", CH)
        conv_out_ready = signal("conv_out_ready", 1)
        gate_cols_ready = signal("gate_cols_ready", 1)
        gates_transposed = signal("gates_transposed", 1)
        gates_ready = signal("gates_ready", 1)
        q_padded = signal("q_padded", ATT)
        scores_done = signal("scores_done", ATT)
        neg_m_ready = signal("neg_m_ready", ATT)
        probs_ready = signal("probs_ready", ATT)
        recip_ready = signal("recip_ready", ATT)
        prob1_scaled = signal("prob1_scaled", ATT)
        a_ready = signal("a_ready", ATT)
        a_transposed = signal("a_transposed", ATT)
        a_col_ready = signal("a_col_ready", ATT)
        pv_done = signal("pv_done", ATT)
        o_copied = signal("o_copied", ATT)
        o_mean_sq_ready = signal("o_mean_sq_ready", TILES)
        o_rstd_ready = signal("o_rstd_ready", TILES)
        o_normed = signal("o_normed", TILES)
        o_transposed = signal("o_transposed", TILES)
        o_mixed = signal("o_mixed", TILES)
        out_done = signal("out_done", TILES - 1)
        x2_ready = signal("x2_ready", TILES)
        ssq2_ready = signal("ssq2_ready", TILES)
        mean_sq2_ready = signal("mean_sq2_ready", TILES)
        rstd2_ready = signal("rstd2_ready", TILES)
        residual_written = [signal(f"residual_written{b}", 3 - b + EXPERTS // 2, 16) for b in range(2)]
        unit_row_ready = signal("unit_row_ready", TILES)
        unit_stored = signal("unit_stored", TILES, 16)
        x2_transposed = signal("x2_transposed", TILES)
        h2_lo_ready = signal("h2_lo_ready", TILES)
        h2_hi_ready = signal("h2_hi_ready", TILES)
        logits_done = signal("logits_done", TILES)
        r_max_ready = signal("r_max_ready", TILES)
        r_exp_ready = signal("r_exp_ready", TILES)
        aff_ready = signal("aff_ready", TILES)
        aff_transposed = signal("aff_transposed", TILES)
        aff_copied = signal("aff_copied", TILES)
        top_ready = signal("top_ready", 1)
        top_transposed = signal("top_transposed", 1)
        result_taken = signal("result_taken", 1 + EXPERTS)
        gathered = [signal(f"gathered{b}", EXPERTS // 2, 16) for b in range(2)]
        picked_transposed = signal("picked_transposed", EXPERTS)
        picked_scaled = signal("picked_scaled", EXPERTS)
        picked_ready = signal("picked_ready", EXPERTS)
        silu_ready = signal("silu_ready", 2 * EXPERTS)
        hid_ready = signal("hid_ready", 2 * EXPERTS)
        gain_loaded = signal("gain_loaded", unit=16)
        fin_loaded = [signal(f"fin_loaded{b}", unit=16) for b in range(2)]
        fin_ssq = signal("fin_ssq")
        fin_mean_sq = signal("fin_mean_sq")
        fin_rstd = signal("fin_rstd")
        fin_normed = signal("fin_normed")
        fin_ready = signal("fin_ready")
        fin_stored = [signal(f"fin_stored{b}", unit=16) for b in range(2)]
        dve_step = signal("dve_step")
        pool_step = signal("pool_step")

        block = ctx.enter_context(nc.Block())

        def tokens(t):
            return slice(t * P, (t + 1) * P)

        def vec(t):
            return 0 if t == 0 else 1

        @block.sync
        def _(sp):
            def dense_unit(l, d, src):
                slot, k = d % DENSE_SLOTS, d // DENSE_SLOTS
                if d >= DENSE_SLOTS:
                    sp.wait_ge(*unit_used.at(l, d - DENSE_SLOTS + 1))
                elif l > 0:
                    sp.wait_ge(*unit_used.at(l - 1, DENSE_UNITS + 6 * (EXPERTS - 1) + d + 1))
                sp.dma_start(ring[:, slot, :].rearrange("p (k n) -> p k n", k=KD), src)\
                  .then_inc(slot_loaded[slot].sem, 16)

            def expert_src(l, e, i):
                if i < 4:
                    w = (w_gate, w_up)[i % 2]
                    return w[l, e].rearrange("(k p) n -> p k n", p=P)[:, :, (i // 2) * BANK:(i // 2 + 1) * BANK]
                return w_down[l, e].rearrange("(k p) n -> p k n", p=P)[:, (i - 4) * 4:(i - 3) * 4, :]

            def expert_unit(l, e, i):
                kk = KD if i < 4 else KD // 2
                sp.dma_start(ring[:, i, :].rearrange("p (k n) -> p k n", k=kk), expert_src(l, e, i))\
                  .then_inc(slot_loaded[i].sem, 16)

            for l in range(DEPTH):
                cols = w_mod[l].rearrange("(k p) n -> p k n", p=P)
                proj = w_in[l].rearrange("(k p) n -> p k n", p=P)
                outw = w_out[l].rearrange("(k p) n -> p k n", p=P)
                order = [(cols, m) for m in range(MOD_FIRST)]
                order += [(proj, m) for m in (0, 1, 3, 2, 4)]
                order += [(cols, m) for m in range(MOD_FIRST, MOD_UNITS)]
                for d, (src, m) in enumerate(order):
                    dense_unit(l, d, src[:, :, m * BANK:(m + 1) * BANK])
                for half in range(OUT_UNITS):
                    d = D_OUT + half
                    sp.wait_ge(*unit_used.at(l, d - DENSE_SLOTS + 1))
                    sp.dma_start(ring[:, d % DENSE_SLOTS, :].rearrange("p (k n) -> p k n", k=KD // 2),
                                 outw[:, half * 4:half * 4 + 4, :]).then_inc(slot_loaded[d % DENSE_SLOTS].sem, 16)
                for i in (0, 3, 4, 5, 1, 2):
                    if i in (0, 3):
                        sp.wait_ge(*unit_used.at(l, D_OUT - (1 if i == 0 else 2) + 1))
                    elif i == 4:
                        sp.wait_ge(*pv_done.at(l, ATT))
                    elif i in (1, 2):
                        sp.wait_ge(*unit_used.at(l, D_OUT + i))
                    expert_unit(l, 0, i)
                with sp.Fori(1, EXPERTS) as e:
                    for i in range(6):
                        sp.wait_ge(*unit_used.at(l, e * 6 + (DENSE_UNITS - 6 + i + 1)))
                        expert_unit(l, e, i)

        @block.tensor
        def _(pe):
            pe.wait_ge(*consts_ready.at(0, 2))
            pe.wait_ge(*cond_loaded.at(0, 2))
            nc.tensor.transpose(ps[:, 0, 0:2 * KD], cond_rows, ident[0:2 * KD, 0:2 * KD])\
              .then_inc(setup_transposed.sem, 1)
            pe.wait_ge(*rows_loaded.at(0, 8 * DEPTH))
            for l in range(DEPTH):
                nc.tensor.transpose(ps[:, 1, l * TAPS * CH:(l + 1) * TAPS * CH], conv_rows[:, l, :],
                                    ident[0:TAPS * CH, 0:TAPS * CH])
                o = DEPTH * TAPS * CH + l * C_ALL
                last = nc.tensor.transpose(ps[:, 1, o:o + C_ALL], par_rows[:, l, :], ident[0:C_ALL, 0:C_ALL])
            last.then_inc(setup_transposed.sem, 1)
            pe.wait_ge(*misc_loaded.at(0, 4 * DEPTH + 3 * DEPTH + 2))
            for l in range(DEPTH):
                for h in range(H):
                    last = nc.tensor.transpose(ps[:, 2 + l, tokens(h)], past_k[:, l, tokens(h)], ident[:])
            last.then_inc(setup_transposed.sem, 1)
            pe.wait_ge(*cond_ready.at(0, 1))

            def wait_unit(l, d):
                pe.wait_ge(*slot_loaded[d % DENSE_SLOTS].at(l, d // DENSE_SLOTS + 1))

            def modulate(l, d, m):
                wait_unit(l, d)
                w = ring[:, d % DENSE_SLOTS, :].rearrange("p (k n) -> p k n", k=KD)
                for b in range(BLK):
                    col = 2 * (m * BLK + b)
                    for k in range(KD):
                        last = nc.tensor.matmul(ps[:, 7, col:col + 2], w[:, k, tokens(b)], cond_silu[:, :, k],
                                                start=(k == 0), stop=(k == KD - 1))
                last.then_inc(unit_used.sem, 1)

            for l in range(DEPTH):
                for m in range(MOD_FIRST):
                    modulate(l, m, m)

                for t in range(TILES):
                    pe.wait_ge(*x_norm_ready.at(l, t + 1))
                    if t >= 2:
                        pe.wait_ge(*h_lo_ready.at(l, t - 1))
                        pe.wait_ge(*h_hi_ready.at(l, t - 1))
                    for k in range(KD):
                        last = nc.tensor.transpose(ps[:, 2 * (t % 2) + k // 4, tokens(k % 4)],
                                                   x_norm[:, tokens(k)], ident[:])
                    last.then_inc(x_transposed.sem, 1)

                pe.wait_ge(*h_lo_ready.at(l, TILES))
                pe.wait_ge(*h_hi_ready.at(l, TILES))
                for i in range(4):
                    d = D_PROJ + i
                    wait_unit(l, d)
                    w = ring[:, d % DENSE_SLOTS, :].rearrange("p (k n) -> p k n", k=KD)
                    for b in range(BLK):
                        n = i * BLK + b
                        if n >= 3:
                            pe.wait_ge(*proj_copied.at(l, n - 2))
                        for bank, cols in ((0, slice(N_CTX, N_TOK)), (1, slice(0, N_CTX))):
                            for k in range(KD):
                                last = nc.tensor.matmul(
                                    ps[:, 2 * (n % 3) + bank, 0:cols.stop - cols.start], w[:, k, tokens(b)],
                                    mix[:, k, cols], start=(k == 0), stop=(k == KD - 1))
                        last.then_inc((unit_used if b == BLK - 1 else proj_done).sem, 1)
                d = D_PROJ + 4
                wait_unit(l, d)
                w = ring[:, d % DENSE_SLOTS, :].rearrange("p (k n) -> p k n", k=KD)
                for t in range(TILES):
                    n = 4 * BLK + t
                    pe.wait_ge(*proj_copied.at(l, n - 2))
                    for k in range(KD):
                        last = nc.tensor.matmul(ps[:, 2 * (n % 3), :], mix[:, k, tokens(t)], w[:, k, :],
                                                start=(k == 0), stop=(k == KD - 1))
                    last.then_inc((unit_used if t == TILES - 1 else proj_done).sem, 1)

                for h in range(H):
                    last = nc.tensor.transpose(ps[:, 6, tokens(h)], k_t[:, h, 0:N_CTX], ident[:])
                last.then_inc(keys_transposed.sem, 1)

                pe.wait_ge(*mod1_ready.at(l, 1))
                for m in range(MOD_FIRST, MOD_UNITS):
                    modulate(l, D_MOD2 + m - MOD_FIRST, m)

                pe.wait_ge(*proj_copied.at(l, 4 * BLK + TILES))
                pe.wait_ge(*conv_ready.at(l, CH - 1))
                pe.wait_ge(*conv3_ready.at(l, 1))
                for c0, c1, bank in ((0, BANK, 0), (BANK, C_LEN, 1)):
                    for j in range(CH):
                        last = nc.tensor.matmul(ps[:, bank, 0:c1 - c0], ones[:], acc[:, j, c0:c1],
                                                start=(j == 0), stop=(j == CH - 1))
                last.then_inc(mean_ready.sem, 1)
                for j in range(CH):
                    pe.wait_ge(*squared.at(l, j + 1))
                    for c0, c1, bank in ((0, BANK, 2), (BANK, C_LEN, 3)):
                        last = nc.tensor.matmul(ps[:, bank, 0:c1 - c0], ones[:], conv_tmp[:, j % 2, c0:c1],
                                                start=(j == 0), stop=(j == CH - 1))
                    last.then_inc(square_used.sem, 1)
                pe.wait_ge(*gate_cols_ready.at(l, 1))
                pe.wait_ge(*conv_normed.at(l, CH))
                for v in range(2):
                    for k in range(KD):
                        nc.tensor.transpose(ps[:, 2 * v + k // 4, tokens(k % 4)], gate1_cols[:, v, k, :], ident[:])
                for k in range(KD):
                    last = nc.tensor.transpose(ps[0:CAP, 4 + k // 4, tokens(k % 4)], gate2_cols[:, k, :], ident[:])
                last.then_inc(gates_transposed.sem, 1)

                def scores(s):
                    t, h = s // H, s % H
                    b0 = 3 * (s % 2)
                    pe.wait_ge(*q_padded.at(l, s + 1))
                    if s >= 2:
                        pe.wait_ge(*probs_ready.at(l, s - 1))
                    for m in range(2):
                        q = q_pad[:, s % 2, m, :]
                        if t > 0:
                            nc.tensor.matmul(ps[:, b0 + m, :], q, k_t[:, h, N_CTX:N_TOK], start=True, stop=True)
                        keys = past_k_t[:, l, h, :] if t > 0 else k_t[:, h, 0:N_CTX]
                        last = nc.tensor.matmul(ps[:, b0 + 2, tokens(m)], q, keys, start=True, stop=True)
                    last.then_inc(scores_done.sem, 1)

                def o_transposes(t):
                    pe.wait_ge(*o_normed.at(l, t + 1))
                    for h in range(H):
                        last = nc.tensor.transpose(ps[:, 6, tokens(h)], o_tok[:, t % 2, h, :], ident[:])
                    last.then_inc(o_transposed.sem, 1)

                pe.wait_ge(*gates_ready.at(l, 1))
                pe.wait_ge(*mod2_ready.at(l, 1))
                pe.wait_ge(*keys_copied.at(l, 1))
                scores(0)
                for s in range(ATT):
                    t, h = s // H, s % H
                    if s + 1 < ATT:
                        scores(s + 1)
                    pe.wait_ge(*a_ready.at(l, s + 1))
                    if s > 0:
                        pe.wait_ge(*o_copied.at(l, s))
                    if t > 0 and h == 2:
                        pe.wait_ge(*o_mixed.at(l, t))
                    tiles = range(1) if t == 0 else range(TILES)
                    for j in tiles:
                        dst = ps[:, 6, tokens(j)] if j < 4 else ps[:, 7, 0:P]
                        last = nc.tensor.transpose(dst, a_row[:, s % 2, tokens(j)], ident[:])
                    last.then_inc(a_transposed.sem, 1)
                    pe.wait_ge(*a_col_ready.at(l, s + 1))
                    for j in tiles:
                        if t == 0:
                            vals = v_tok[:, 0, tokens(h)]
                        else:
                            vals = v_tok[:, j + 1, tokens(h)] if j < 4 else past_v[:, l, tokens(h)]
                        last = nc.tensor.matmul(ps[:, 7, 2 * P:3 * P], a_col[:, tokens(j)], vals,
                                                start=(j == 0), stop=(j == len(tiles) - 1))
                    last.then_inc(pv_done.sem, 1)
                    if t > 0 and h == 1:
                        o_transposes(t - 1)
                o_transposes(TILES - 1)

                def out_tile(t):
                    if t >= 2:
                        pe.wait_ge(*x2_ready.at(l, t - 1))
                    for k in range(KD):
                        d = D_OUT + k // 4
                        if t == 0 and k % 4 == 0:
                            wait_unit(l, d)
                        w = ring[:, d % DENSE_SLOTS, :].rearrange("p (k n) -> p k n", k=KD // 2)
                        for n in range(2):
                            last = nc.tensor.matmul(ps[:, 2 * (t % 2) + n, :], mix[:, k, tokens(t)],
                                                    w[:, k % 4, n * BANK:(n + 1) * BANK],
                                                    start=(k == 0), stop=(k == KD - 1))
                        if t == TILES - 1 and k == 3:
                            last.then_inc(unit_used.sem, 1)
                    last.then_inc((unit_used if t == TILES - 1 else out_done).sem, 1)

                def x2_transposes(t):
                    pe.wait_ge(*unit_row_ready.at(l, t + 1))
                    for k in range(KD):
                        last = nc.tensor.transpose(ps[:, 4 + k // 4, tokens(k % 4)], x_norm[:, tokens(k)], ident[:])
                    last.then_inc(x2_transposed.sem, 1)

                def logits(t):
                    pe.wait_ge(*h2_lo_ready.at(l, t + 1))
                    pe.wait_ge(*h2_hi_ready.at(l, t + 1))
                    for k in range(KD):
                        last = nc.tensor.matmul(ps[:, 6, 0:EXPERTS], h2_t[:, k, :], router[:, l, k, :],
                                                start=(k == 0), stop=(k == KD - 1))
                    last.then_inc(logits_done.sem, 1)

                def aff_transpose(t):
                    pe.wait_ge(*aff_ready.at(l, t + 1))
                    if t > 0:
                        pe.wait_ge(*aff_copied.at(l, t))
                    nc.tensor.transpose(ps[0:EXPERTS, 7, 0:P], aff[:], ident[:]).then_inc(aff_transposed.sem, 1)

                pe.wait_ge(*o_mixed.at(l, TILES))
                pe.wait_ge(*conv_out_ready.at(l, 1))
                out_tile(0)
                for t in range(TILES):
                    if t + 1 < TILES:
                        out_tile(t + 1)
                    x2_transposes(t)
                    if t > 0:
                        aff_transpose(t - 1)
                    logits(t)
                aff_transpose(TILES - 1)

                pe.wait_ge(*top_ready.at(l, 1))
                nc.tensor.transpose(ps[0:CAP, 4, 0:EXPERTS], top_f, ident[0:EXPERTS, 0:EXPERTS])
                nc.tensor.transpose(ps[0:CAP, 5, 0:EXPERTS], top_v, ident[0:EXPERTS, 0:EXPERTS])\
                  .then_inc(top_transposed.sem, 1)
                pe.wait_ge(*result_taken.at(l, 1))

                def picked_transposes(e, b, rnd):
                    pe.wait_ge(*gathered[b].at(l, rnd + 1))
                    for k in range(KD):
                        last = nc.tensor.transpose(ps[:, 6 + k // 4, (k % 4) * CAP:(k % 4 + 1) * CAP],
                                                   picked[:, b, tokens(k)], ident[0:CAP, 0:CAP])
                    last.then_inc(picked_transposed.sem, 1)

                def gate_up(e, b):
                    pe.wait_ge(*picked_ready.at(l, e + 1))
                    for i in range(4):
                        pe.wait_ge(*slot_loaded[i].at(l, e + (slot_dense[i] + 1)))
                        w = ring[:, i, :].rearrange("p (k n) -> p k n", k=KD)
                        for f in range(BLK):
                            for k in range(KD):
                                last = nc.tensor.matmul(ps[:, i, f * CAP:(f + 1) * CAP], w[:, k, tokens(f)],
                                                        picked_t[:, b, k, :], start=(k == 0), stop=(k == KD - 1))
                        last.then_inc(unit_used.sem, 1)

                def down(e):
                    pe.wait_ge(*result_taken.at(l, e + 1))
                    for half in range(2):
                        pe.wait_ge(*slot_loaded[4 + half].at(l, e + 1))
                        pe.wait_ge(*hid_ready.at(l, 2 * e + half + 1))
                        w = ring[:, 4 + half, :].rearrange("p (k n) -> p k n", k=KD // 2)
                        for kk in range(KD // 2):
                            k = half * (KD // 2) + kk
                            for n in range(2):
                                last = nc.tensor.matmul(ps[0:CAP, 4 + n, :], hid[:, k, :],
                                                        w[:, kk, n * BANK:(n + 1) * BANK],
                                                        start=(k == 0), stop=(k == KD - 1))
                        last.then_inc(unit_used.sem, 1)

                with pe.Fori(0, EXPERTS // 2) as r:
                    picked_transposes(r * 2, 0, r)
                    gate_up(r * 2, 0)
                    picked_transposes(r * 2 + 1, 1, r)
                    down(r * 2)
                    gate_up(r * 2 + 1, 1)
                    down(r * 2 + 1)

        @block.scalar
        def _(act):
            act.dma_start(cond_rows[0:KD, :], c_ctx.rearrange("(k p) -> k p", p=P)).then_inc(cond_loaded.sem, 16)
            act.dma_start(cond_rows[KD:2 * KD, :], c[0].rearrange("(k p) -> k p", p=P)).then_inc(cond_loaded.sem, 16)
            for l in range(DEPTH):
                act.dma_start(conv_rows[:, l, :], conv_w[l].rearrange("t (k p) -> (t k) p", p=P))\
                   .then_inc(rows_loaded.sem, 16)
                for src, at in ((b_mod, C_BMOD), (norm1_g, C_N1), (norm2_g, C_N2), (conv_b, C_CB),
                                (conv_ln_g, C_LG), (conv_ln_b, C_LB), (subln_g, C_SUB)):
                    n = src.shape[1] // P
                    act.dma_start(par_rows[at:at + n, l, :], src[l].rearrange("(k p) -> k p", p=P))\
                       .then_inc(rows_loaded.sem, 16)
            for l in range(DEPTH):
                for f, src in enumerate((lambda_q1, lambda_k1, lambda_q2, lambda_k2)):
                    act.dma_start(lam_rows[:, l, f, :], src[l:l + 1, :].to_broadcast([P, HD]))\
                       .then_inc(misc_loaded.sem, 16)
                act.dma_start(past_k[:, l, :], cache_k[0, l].rearrange("t h c d -> t (h c d)"))\
                   .then_inc(misc_loaded.sem, 16)
                act.dma_start(past_v[:, l, :], cache_v[0, l].rearrange("t h d -> t (h d)"))\
                   .then_inc(misc_loaded.sem, 16)
                act.dma_start(router[:, l], w_router[l].rearrange("(k p) e -> p k e", p=P))\
                   .then_inc(misc_loaded.sem, 16)
            act.dma_start(cos_sb[:], rope_cos).then_inc(misc_loaded.sem, 16)
            act.dma_start(sin_sb[:], rope_sin).then_inc(misc_loaded.sem, 16)

            act.wait_ge(*setup_transposed.at(0, 1))
            nc.scalar.activation(cond_silu[:].rearrange("p v k -> p (v k)"), ps[:, 0, 0:2 * KD], ACT.Silu)\
              .then_inc(cond_ready.sem, 1)
            act.wait_ge(*lam_summed.at(0, 1))
            nc.scalar.activation(lam_e[:], lam_e[:], ACT.Exp).then_inc(lam_exped.sem, 1)

            for l in range(DEPTH):
                def h_hi(t):
                    act.wait_ge(*x_transposed.at(l, t + 1))
                    if t == 0:
                        act.wait_ge(*mod1_ready.at(l, 1))
                    for k in range(4, KD):
                        last = nc.scalar.activation(mix[:, k, tokens(t)], ps[:, 2 * (t % 2) + 1, tokens(k - 4)],
                                                    ACT.Identity, scale=scale1[:, k, vec(t):vec(t) + 1],
                                                    bias=mod[:, k, vec(t):vec(t) + 1])
                    last.then_inc(h_hi_ready.sem, 1)

                for t in range(TILES):
                    act.wait_ge(*x_loaded[t % 2].at(l, t // 2 + 1))
                    if t > 0:
                        act.wait_ge(*x_transposed.at(l, t))
                    nc.scalar.activation(x_norm[:], x_tile[:, t % 2, :], ACT.Square, accum_out=ssq[:, 0:1])\
                      .then_inc(ssq_ready.sem, 1)
                    act.wait_ge(*rstd_ready.at(l, t + 1))
                    nc.scalar.activation(x_norm[:], x_tile[:, t % 2, :], ACT.Copy, scale=rstd[:, 0:1])\
                      .then_inc(x_norm_ready.sem, 1)
                    if t > 0:
                        h_hi(t - 1)
                h_hi(TILES - 1)

                for n in range(4 * BLK):
                    i, b = n // BLK, n % BLK
                    lat, con = ps[:, 2 * (n % 3), :], ps[:, 2 * (n % 3) + 1, 0:N_CTX]
                    if b == BLK - 1:
                        act.wait_ge(*unit_used.at(l, D_PROJ + i + 1))
                    else:
                        act.wait_ge(*proj_done.at(l, i * (BLK - 1) + b + 1))
                    if i == 0:
                        if b == 0:
                            act.wait_ge(*halo_zero.at(l, 1))
                        nc.scalar.activation(u[:, b, HALO + LAT0:HALO + LAT0 + N_LAT], lat, ACT.Copy)
                        last = nc.scalar.activation(u[:, b, HALO:HALO + N_CTX], con, ACT.Copy)
                    elif i == 1:
                        if b >= 2:
                            act.wait_ge(*glu_ready.at(l, b - 1))
                        nc.scalar.activation(conv_tmp[:, b % 2, LAT0:C_LEN], lat, ACT.Sigmoid)
                        last = nc.scalar.activation(conv_tmp[:, b % 2, 0:N_CTX], con, ACT.Sigmoid)
                    else:
                        dst = k_t if i == 2 else q_t
                        nc.scalar.activation(dst[:, b, N_CTX:N_TOK], lat, ACT.Copy)
                        last = nc.scalar.activation(dst[:, b, 0:N_CTX], con, ACT.Copy)
                    last.then_inc(proj_copied.sem, 1)
                for t in range(TILES):
                    n = 4 * BLK + t
                    if t == TILES - 1:
                        act.wait_ge(*unit_used.at(l, D_MOD2))
                    else:
                        act.wait_ge(*proj_done.at(l, 4 * (BLK - 1) + t + 1))
                    nc.scalar.activation(v_tok[:, t, :], ps[:, 2 * (n % 3), :], ACT.Copy).then_inc(proj_copied.sem, 1)
                act.wait_ge(*proj_copied.at(l, 4 * BLK + 1))
                act.dma_start(new_cache_v[0, l].rearrange("t h d -> t (h d)"), v_tok[:, 0, :])\
                   .then_inc(cache_stored.sem, 16)
                act.wait_ge(*keys_transposed.at(l, 1))
                act.wait_ge(*glu_ready.at(l, CH))
                nc.scalar.activation(key_rows, ps[:, 6, :], ACT.Copy).then_inc(keys_copied.sem, 1)
                act.wait_ge(*keys_copied.at(l, 1))
                act.dma_start(new_cache_k[0, l].rearrange("t h c d -> t (h c d)"), key_rows)\
                   .then_inc(cache_stored.sem, 16)
                act.wait_ge(*cache_stored.at(l, 2))

                for j in range(CH):
                    act.wait_ge(*centred.at(l, j + 1))
                    if j >= 2:
                        act.wait_ge(*square_used.at(l, j - 1))
                    nc.scalar.activation(conv_tmp[:, j % 2, :], acc[:, j, :], ACT.Square).then_inc(squared.sem, 1)
                act.wait_ge(*square_used.at(l, CH))
                nc.scalar.activation(conv_rstd, ps[:, 2:4, :].rearrange("p b n -> p (b n)")[:, 0:C_LEN], ACT.Sqrt,
                                     scale=1.0 / D_CONV, bias=eps[:]).then_inc(conv_std_ready.sem, 1)
                for j in range(CH):
                    act.wait_ge(*conv_normed.at(l, j + 1))
                    for cols, src in ((slice(0, N_CTX), slice(0, N_CTX)), (slice(N_CTX, N_TOK), slice(LAT0, C_LEN))):
                        last = nc.scalar.activation(mix[:, j, cols], acc[:, j, src], ACT.Silu,
                                                    scale=par_cols[:, l, C_LG + j:C_LG + j + 1],
                                                    bias=par_cols[:, l, C_LB + j:C_LB + j + 1])
                last.then_inc(conv_out_ready.sem, 1)
                act.wait_ge(*gates_transposed.at(l, 1))
                for v in range(2):
                    for n in range(2):
                        nc.scalar.activation(gate1[:, v, n * BANK:(n + 1) * BANK], ps[:, 2 * v + n, :], ACT.Copy)
                for n in range(2):
                    last = nc.scalar.activation(gate2[:, n * BANK:(n + 1) * BANK], ps[0:CAP, 4 + n, :], ACT.Copy)
                last.then_inc(gates_ready.sem, 1)

                def exps(s):
                    t, b0, b = s // H, 3 * (s % 2), s % 2
                    act.wait_ge(*neg_m_ready.at(l, s + 1))
                    for m in range(2):
                        if t > 0:
                            nc.scalar.activation(prob[:, b, m, 0:N_LAT], ps[:, b0 + m, :], ACT.Exp,
                                                 bias=neg_m[:, b, m:m + 1], accum_out=row_sum[:, b, 0, m:m + 1])
                        at = N_LAT if t > 0 else 0
                        last = nc.scalar.activation(prob[:, b, m, at:at + P], ps[:, b0 + 2, tokens(m)], ACT.Exp,
                                                    bias=neg_m[:, b, m:m + 1], accum_out=row_sum[:, b, 1, m:m + 1])
                    last.then_inc(probs_ready.sem, 1)

                exps(0)
                for s in range(ATT):
                    t, h, b = s // H, s % H, s % 2
                    n = N_TOK if t > 0 else N_CTX
                    act.wait_ge(*recip_ready.at(l, s + 1))
                    nc.scalar.activation(prob[:, b, 1, 0:n], prob[:, b, 1, 0:n], ACT.Copy, scale=row_r[:, b, 1:2])\
                      .then_inc(prob1_scaled.sem, 1)
                    if s + 1 < ATT:
                        exps(s + 1)
                    act.wait_ge(*a_transposed.at(l, s + 1))
                    if s > 0:
                        act.wait_ge(*pv_done.at(l, s))
                    if t > 0:
                        nc.scalar.activation(a_col[:, 0:N_LAT], ps[:, 6, :], ACT.Copy)
                        last = nc.scalar.activation(a_col[:, N_LAT:N_TOK], ps[:, 7, 0:P], ACT.Copy)
                    else:
                        last = nc.scalar.activation(a_col[:, 0:P], ps[:, 6, 0:P], ACT.Copy)
                    last.then_inc(a_col_ready.sem, 1)
                    done = t - 1 if (t > 0 and h == 1) else TILES - 1 if s == ATT - 1 else None
                    if done is not None:
                        act.wait_ge(*o_transposed.at(l, done + 1))
                        nc.scalar.activation(mix[:, CH:KD, tokens(done)],
                                             ps[:, 6, :].rearrange("p (h n) -> p h n", h=H), ACT.Copy,
                                             scale=sub_cols[:, l:l + 1]).then_inc(o_mixed.sem, 1)

                def h2_hi(t):
                    act.wait_ge(*x2_transposed.at(l, t + 1))
                    if t > 0:
                        act.wait_ge(*logits_done.at(l, t))
                    for k in range(4, KD):
                        last = nc.scalar.activation(h2_t[:, k, :], ps[:, 5, tokens(k - 4)], ACT.Identity,
                                                    scale=scale2[:, k, vec(t):vec(t) + 1],
                                                    bias=mod[:, 3 * KD + k, vec(t):vec(t) + 1])
                    last.then_inc(h2_hi_ready.sem, 1)

                def router_exp(t):
                    act.wait_ge(*r_max_ready.at(l, t + 1))
                    nc.scalar.activation(r_exp[:], ps[:, 6, 0:EXPERTS], ACT.Exp, bias=r_max[:],
                                         accum_out=r_sum[:]).then_inc(r_exp_ready.sem, 1)

                for t in range(TILES):
                    act.wait_ge(*x2_ready.at(l, t + 1))
                    if t > 0:
                        act.wait_ge(*unit_stored.at(l, t))
                        act.wait_ge(*x2_transposed.at(l, t))
                    nc.scalar.activation(x_norm[:], x_tile[:, t % 2, :], ACT.Square, accum_out=ssq[:, 1:2])\
                      .then_inc(ssq2_ready.sem, 1)
                    act.wait_ge(*rstd2_ready.at(l, t + 1))
                    nc.scalar.activation(x_norm[:], x_tile[:, t % 2, :], ACT.Copy, scale=rstd[:, 1:2])\
                      .then_inc(unit_row_ready.sem, 1)
                    act.wait_ge(*unit_row_ready.at(l, t + 1))
                    act.dma_start(x_unit[tokens(t), :], x_norm[:]).then_inc(unit_stored.sem, 16)
                    h2_hi(t)
                    router_exp(t)

                with act.Fori(0, EXPERTS) as e:
                    for half in range(2):
                        act.wait_ge(*unit_used.at(l, e * 6 + (DENSE_UNITS + 2 * half + 1)))
                        nc.scalar.activation(silu_g[:, half, 0:BLK * CAP], ps[:, 2 * half, 0:BLK * CAP], ACT.Silu)\
                          .then_inc(silu_ready.sem, 1)

            for t in range(TILES):
                b = t % 2
                act.wait_ge(*fin_loaded[b].at(0, t // 2 + 1))
                if t > 0:
                    act.wait_ge(*fin_ready.at(0, t))
                nc.scalar.activation(x_norm[:], x_tile[:, b, :], ACT.Square, accum_out=ssq[:, 2:3])\
                  .then_inc(fin_ssq.sem, 1)
                act.wait_ge(*fin_rstd.at(0, t + 1))
                nc.scalar.activation(x_norm[:], x_tile[:, b, :], ACT.Copy, scale=rstd[:, 2:3])\
                  .then_inc(fin_normed.sem, 1)
                act.wait_ge(*fin_ready.at(0, t + 1))
                dst = y_prompt[0] if t == 0 else y_sample[0, (t - 1) * P:t * P, :]
                act.dma_start(dst, x_tile[:, b, :]).then_inc(fin_stored[b].sem, 16)
            act.wait_ge(*fin_stored[0].at(0, 3))
            act.wait_ge(*fin_stored[1].at(0, 2))
            act.wait_ge(*cache_stored.at(DEPTH - 1, 2))

        @block.vector
        def _(dve):
            steps = [0]

            def step(ins):
                ins.then_inc(dve_step.sem, 1)
                steps[0] += 1
                return steps[0]

            def own(n):
                dve.wait_ge(dve_step.sem, n)

            dve.wait_ge(*misc_loaded.at(0, 4 * DEPTH + 3 * DEPTH + 2))
            own(step(nc.vector.tensor_tensor(lam_prod, lam_rows[:, :, 0:4:2, :], lam_rows[:, :, 1:4:2, :], ALU.mult)))
            nc.vector.tensor_reduce(lam_e[:], lam_prod, AX, ALU.add).then_inc(lam_summed.sem, 1)
            dve.wait_ge(*setup_transposed.at(0, 3))
            nc.vector.tensor_copy(conv_cols[:].rearrange("p l n -> p (l n)"), ps[:, 1, 0:DEPTH * TAPS * CH])
            nc.vector.tensor_copy(par_cols[:].rearrange("p l n -> p (l n)"),
                                  ps[:, 1, DEPTH * TAPS * CH:DEPTH * (TAPS * CH + C_ALL)])
            own(step(nc.vector.tensor_copy(past_k_t[:].rearrange("p l h n -> p l (h n)"), ps[:, 2:2 + DEPTH, :])))
            dve.wait_ge(*lam_exped.at(0, 1))
            for l in range(DEPTH):
                nc.vector.tensor_scalar(lam[:, l:l + 1], lam_e[:, l, 0:1], lam_e[:, l, 1:2], lam_init[l],
                                        ALU.subtract, ALU.add)
                last = nc.vector.tensor_scalar(sub_cols[:, l:l + 1], par_cols[:, l, C_SUB:C_SUB + 1],
                                               1.0 - lam_init[l], None, ALU.mult)
            own(step(last))
            own(step(nc.vector.memset(map_scale[:], 0.0)))
            for m in range(2):
                last = nc.vector.memset(map_scale[m * HD:(m + 1) * HD, m:m + 1], HD ** -0.5)
            last.then_inc(setup_copied.sem, 1)

            for l in range(DEPTH):
                def mean_square(col, ready):
                    nc.vector.tensor_scalar(mean_sq[:, col:col + 1], ssq[:, col:col + 1], 1.0 / D, EPS,
                                            ALU.mult, ALU.add).then_inc(ready.sem, 1)

                def take_mod(u0, u1):
                    lo, hi = u0 * BLK, u1 * BLK
                    bias = par_cols[:, l, C_BMOD + lo:C_BMOD + hi].unsqueeze(2).to_broadcast([P, hi - lo, 2])
                    own(step(nc.vector.tensor_tensor(
                        mod[:, lo:hi, :], ps[:, 7, 2 * lo:2 * hi].rearrange("p (n v) -> p n v", v=2), bias, ALU.add)))

                def gain(dst, q, at):
                    g = par_cols[:, l, at:at + KD].unsqueeze(2).to_broadcast([P, KD, 2])
                    return nc.vector.scalar_tensor_tensor(dst[:], mod[:, q * KD:(q + 1) * KD, :], 1.0, g,
                                                          ALU.add, ALU.mult)

                def h_lo(t):
                    dve.wait_ge(*x_transposed.at(l, t + 1))
                    for k in range(4):
                        v = vec(t)
                        last = nc.vector.tensor_scalar(mix[:, k, tokens(t)], ps[:, 2 * (t % 2), tokens(k)],
                                                       scale1[:, k, v:v + 1], mod[:, k, v:v + 1],
                                                       ALU.mult, ALU.add)
                    last.then_inc(h_lo_ready.sem, 1)

                dve.wait_ge(*ssq_ready.at(l, 1))
                mean_square(0, mean_sq_ready)
                dve.wait_ge(*unit_used.at(l, MOD_FIRST))
                take_mod(0, MOD_FIRST)
                gain(scale1, 1, C_N1).then_inc(mod1_ready.sem, 1)
                dve.wait_ge(*mod1_ready.at(l, 1))
                for t in range(1, TILES):
                    dve.wait_ge(*ssq_ready.at(l, t + 1))
                    mean_square(0, mean_sq_ready)
                    h_lo(t - 1)
                h_lo(TILES - 1)

                for b in range(CH):
                    dve.wait_ge(*proj_copied.at(l, BLK + b + 1))
                    for ucol, col, n in ((HALO, 0, N_CTX), (HALO + LAT0, LAT0, N_LAT)):
                        dst = u[:, b, ucol:ucol + n]
                        last = nc.vector.tensor_tensor(dst, dst, conv_tmp[:, b % 2, col:col + n], ALU.mult)
                    last.then_inc(glu_ready.sem, 1)
                dve.wait_ge(*glu_ready.at(l, CH))

                done = [0] * (CH - 1)

                def taps(t0, t1):
                    for t in range(t0, t1):
                        for j in range(CH - 1):
                            w = conv_cols[:, l, t * CH + j:t * CH + j + 1]
                            src = u[:, j, t:t + C_LEN]
                            if t == 0:
                                ins = nc.vector.tensor_scalar(acc[:, j, :], src, w,
                                                              par_cols[:, l, C_CB + j:C_CB + j + 1],
                                                              ALU.mult, ALU.add)
                            else:
                                own(done[j])
                                ins = nc.vector.scalar_tensor_tensor(acc[:, j, :], src, w, acc[:, j, :],
                                                                     ALU.mult, ALU.add)
                            if t == TAPS - 1:
                                ins.then_inc(conv_ready.sem, 1)
                            else:
                                done[j] = step(ins)

                def swaps(i):
                    for h in range(H):
                        dve.wait_ge(*proj_copied.at(l, (2 + i) * BLK + h + 1))
                        src = (k_t, q_t)[i][:, h, N_CTX:N_TOK]
                        nc.vector.stream_shuffle(rope_tmp[:, i * H + h, :], src, [p ^ 16 for p in range(32)])\
                          .then_inc(rope_shuffled.sem, 1)

                taps(0, TAPS // 2)
                swaps(0)
                taps(TAPS // 2, TAPS)
                swaps(1)

                dve.wait_ge(*mean_ready.at(l, 1))
                mean = ps[:, 0:2, :].rearrange("p b n -> p (b n)")[:, 0:C_LEN]
                for j in range(CH):
                    nc.vector.scalar_tensor_tensor(acc[:, j, :], mean, -1.0 / D_CONV, acc[:, j, :],
                                                   ALU.mult, ALU.add).then_inc(centred.sem, 1)
                dve.wait_ge(*unit_used.at(l, D_OUT))
                take_mod(MOD_FIRST, MOD_UNITS)
                own(step(gain(scale2, 4, C_N2)))
                for dst, q, src in ((shift2_x, 3, mod), (scale2_x, 0, scale2)):
                    cols = src[:, q * KD:(q + 1) * KD, :]
                    nc.vector.tensor_copy(dst[:, :, 0:CAP_LAT], cols[:, :, 1:2].to_broadcast([P, KD, CAP_LAT]))
                    last = nc.vector.tensor_copy(dst[:, :, CAP_LAT:CAP],
                                                 cols[:, :, 0:1].to_broadcast([P, KD, CAP_CTX]))
                last.then_inc(mod2_ready.sem, 1)
                dve.wait_ge(*conv_std_ready.at(l, 1))
                own(step(nc.vector.reciprocal(conv_rstd, conv_rstd)))
                for j in range(CH):
                    nc.vector.tensor_tensor(acc[:, j, :], acc[:, j, :], conv_rstd, ALU.mult)\
                      .then_inc(conv_normed.sem, 1)
                dve.wait_ge(*conv_out_ready.at(l, 1))
                for v in range(2):
                    nc.vector.tensor_copy(gate1_cols[:, v], mod[:, 2 * KD:3 * KD, v:v + 1].to_broadcast([P, KD, P]))
                g2 = mod[:, 5 * KD:6 * KD, :]
                nc.vector.tensor_copy(gate2_cols[:, :, 0:CAP_LAT], g2[:, :, 1:2].to_broadcast([P, KD, CAP_LAT]))
                nc.vector.tensor_copy(gate2_cols[:, :, CAP_LAT:CAP], g2[:, :, 0:1].to_broadcast([P, KD, CAP_CTX]))\
                  .then_inc(gate_cols_ready.sem, 1)

                def row_max(s):
                    t, b0, b = s // H, 3 * (s % 2), s % 2
                    dve.wait_ge(*scores_done.at(l, s + 1))
                    tail = ps[:, b0 + 2, 0:2 * P].rearrange("p (m n) -> p m n", m=2)
                    if t > 0:
                        nc.vector.tensor_reduce(neg_max[:, b, 0, :], ps[:, b0:b0 + 2, :], AX, ALU.max, negate=True)
                        own(step(nc.vector.tensor_reduce(neg_max[:, b, 1, :], tail, AX, ALU.max, negate=True)))
                        nc.vector.tensor_tensor(neg_m[:, b, :], neg_max[:, b, 0, :], neg_max[:, b, 1, :], ALU.min)\
                          .then_inc(neg_m_ready.sem, 1)
                    else:
                        nc.vector.tensor_reduce(neg_m[:, b, :], tail, AX, ALU.max, negate=True)\
                          .then_inc(neg_m_ready.sem, 1)

                def o_norm(t):
                    b = t % 2
                    own(step(nc.vector.tensor_tensor(o_sq[:], o_tok[:, b], o_tok[:, b], ALU.mult)))
                    own(step(nc.vector.tensor_reduce(o_ss[:, b, :], o_sq[:], AX, ALU.add)))
                    nc.vector.tensor_scalar(o_ss[:, b, :], o_ss[:, b, :], 1.0 / VD, EPS, ALU.mult, ALU.add)\
                      .then_inc(o_mean_sq_ready.sem, 1)

                def o_scale(t):
                    b = t % 2
                    dve.wait_ge(*o_rstd_ready.at(l, t + 1))
                    nc.vector.tensor_tensor(o_tok[:, b], o_tok[:, b],
                                            o_rstd[:, b, :].unsqueeze(2).to_broadcast([P, H, VD]), ALU.mult)\
                      .then_inc(o_normed.sem, 1)

                def take_o(s):
                    dve.wait_ge(*pv_done.at(l, s + 1))
                    nc.vector.tensor_copy(o_tok[:, (s // H) % 2, s % H, :], ps[:, 7, 2 * P:3 * P])\
                      .then_inc(o_copied.sem, 1)
                    if s % H == H - 1:
                        dve.wait_ge(*o_copied.at(l, s + 1))
                        o_norm(s // H)

                row_max(0)
                for s in range(ATT):
                    t, b = s // H, s % 2
                    n = N_TOK if t > 0 else N_CTX
                    dve.wait_ge(*probs_ready.at(l, s + 1))
                    if t > 0:
                        own(step(nc.vector.tensor_tensor(row_r[:, b, :], row_sum[:, b, 0, :], row_sum[:, b, 1, :],
                                                         ALU.add)))
                        own(step(nc.vector.reciprocal(row_r[:, b, :], row_r[:, b, :])))
                    else:
                        own(step(nc.vector.reciprocal(row_r[:, b, :], row_sum[:, b, 1, :])))
                    nc.vector.tensor_tensor(row_r[:, b, 1:2], row_r[:, b, 1:2], lam[:, l:l + 1], ALU.mult)\
                      .then_inc(recip_ready.sem, 1)
                    if s > H and s % H == 1:
                        o_scale(s // H - 1)
                    if s > 0:
                        take_o(s - 1)
                    if s + 1 < ATT:
                        row_max(s + 1)
                    dve.wait_ge(*prob1_scaled.at(l, s + 1))
                    nc.vector.scalar_tensor_tensor(a_row[:, b, 0:n], prob[:, b, 0, 0:n], row_r[:, b, 0:1],
                                                   prob[:, b, 1, 0:n], ALU.mult, ALU.subtract)\
                      .then_inc(a_ready.sem, 1)
                take_o(ATT - 1)
                o_scale(TILES - 1)

                out_tmp = conv_tmp[:, :, :].rearrange("p b n -> p (b n)")[:, 0:D]

                def x2(t):
                    if t == TILES - 1:
                        dve.wait_ge(*unit_used.at(l, DENSE_UNITS))
                    else:
                        dve.wait_ge(*out_done.at(l, t + 1))
                    y = ps[:, 2 * (t % 2):2 * (t % 2) + 2, :].rearrange("p b n -> p (b n)")
                    b = t % 2
                    own(step(nc.vector.tensor_tensor(out_tmp, y, gate1[:, vec(t), :], ALU.mult)))
                    dve.wait_ge(*x_loaded[b].at(l, 3 - b + t // 2 + 1))
                    nc.vector.tensor_tensor(x_tile[:, b, :], x_tile[:, b, :], out_tmp, ALU.add)\
                      .then_inc(x2_ready.sem, 1)

                def h2_lo(t):
                    dve.wait_ge(*x2_transposed.at(l, t + 1))
                    if t > 0:
                        dve.wait_ge(*logits_done.at(l, t))
                    v = vec(t)
                    for k in range(4):
                        last = nc.vector.tensor_scalar(h2_t[:, k, :], ps[:, 4, tokens(k)], scale2[:, k, v:v + 1],
                                                       mod[:, 3 * KD + k, v:v + 1], ALU.mult, ALU.add)
                    last.then_inc(h2_lo_ready.sem, 1)

                def take_aff(t):
                    dve.wait_ge(*aff_transposed.at(l, t + 1))
                    nc.vector.tensor_copy(aff_t[:, tokens(t)], ps[0:EXPERTS, 7, 0:P]).then_inc(aff_copied.sem, 1)

                for t in range(TILES):
                    x2(t)
                    dve.wait_ge(*ssq2_ready.at(l, t + 1))
                    mean_square(1, mean_sq2_ready)
                    h2_lo(t)
                    if t > 0:
                        take_aff(t - 1)
                    dve.wait_ge(*logits_done.at(l, t + 1))
                    nc.vector.tensor_reduce(r_max[:], ps[:, 6, 0:EXPERTS], AX, ALU.max, negate=True)\
                      .then_inc(r_max_ready.sem, 1)
                    dve.wait_ge(*r_exp_ready.at(l, t + 1))
                    own(step(nc.vector.reciprocal(r_sum[:], r_sum[:])))
                    nc.vector.tensor_scalar(aff[:], r_exp[:], r_sum[:], None, ALU.mult).then_inc(aff_ready.sem, 1)
                take_aff(TILES - 1)

                dve.wait_ge(*aff_copied.at(l, TILES))
                for cols, at, count in ((slice(0, N_CTX), CAP_LAT, CAP_CTX), (slice(N_CTX, N_TOK), 0, CAP_LAT)):
                    left = aff_t[:, cols]
                    for i in range(at, at + count, 8):
                        own(step(nc.vector.max(top_v[:, i:i + 8], left)))
                        nc.vector.max_index(top_i[:, i:i + 8], top_v[:, i:i + 8], left)
                        own(step(nc.vector.match_replace(left, top_v[:, i:i + 8], left, -1.0)))
                own(step(nc.vector.tensor_copy(top_f, top_i)))
                nc.vector.tensor_scalar_add(top_f[:, 0:CAP_LAT], top_f[:, 0:CAP_LAT], float(N_CTX))\
                  .then_inc(top_ready.sem, 1)
                dve.wait_ge(*top_transposed.at(l, 1))
                nc.vector.tensor_copy(row_idx[:], ps[0:CAP, 4, 0:EXPERTS])
                nc.vector.tensor_copy(gsel[:], ps[0:CAP, 5, 0:EXPERTS]).then_inc(result_taken.sem, 1)
                dve.wait_ge(*result_taken.at(l, 1))

                def modulate_picked(e, b):
                    dve.wait_ge(*picked_transposed.at(l, e + 1))
                    dst = picked_t[:, b].rearrange("p (a k) n -> p a (k n)", a=2)
                    sc = scale2_x[:].rearrange("p (a k) n -> p a (k n)", a=2)
                    sh = shift2_x[:].rearrange("p (a k) n -> p a (k n)", a=2)
                    nc.vector.tensor_tensor(dst, ps[:, 6:8, 0:4 * CAP], sc, ALU.mult).then_inc(picked_scaled.sem, 1)
                    dve.wait_ge(*picked_scaled.at(l, e + 1))
                    nc.vector.tensor_tensor(dst, dst, sh, ALU.add).then_inc(picked_ready.sem, 1)

                def gated_hidden(e):
                    for half in range(2):
                        dve.wait_ge(*unit_used.at(l, e * 6 + (DENSE_UNITS + 2 * half + 2)))
                        dve.wait_ge(*silu_ready.at(l, e * 2 + half + 1))
                        dst = hid[:, half * BLK:(half + 1) * BLK, :].rearrange("p k n -> p (k n)")
                        nc.vector.tensor_tensor(dst, silu_g[:, half, 0:BLK * CAP], ps[:, 2 * half + 1, 0:BLK * CAP],
                                                ALU.mult).then_inc(hid_ready.sem, 1)

                def gated_result(e, b, rnd):
                    dve.wait_ge(*unit_used.at(l, e * 6 + (DENSE_UNITS + 6)))
                    dve.wait_ge(*residual_written[b].at(l, rnd + (3 - b)))
                    nc.vector.scalar_tensor_tensor(added[:, b, :], ps[0:CAP, 4:6, :].rearrange("p b n -> p (b n)"),
                                                   gsel[:, bass.ds(e, 1)], gate2[:], ALU.mult, ALU.mult)\
                      .then_inc(result_taken.sem, 1)

                with dve.Fori(0, EXPERTS // 2) as r:
                    modulate_picked(r * 2, 0)
                    gated_hidden(r * 2)
                    modulate_picked(r * 2 + 1, 1)
                    gated_result(r * 2, 0, r)
                    gated_hidden(r * 2 + 1)
                    gated_result(r * 2 + 1, 1, r)

            gain_rows = h2_t.rearrange("p k n -> p (k n)")
            dve.wait_ge(*gain_loaded.at(0, 1))
            for t in range(TILES):
                dve.wait_ge(*fin_ssq.at(0, t + 1))
                nc.vector.tensor_scalar(mean_sq[:, 2:3], ssq[:, 2:3], 1.0 / D, EPS, ALU.mult, ALU.add)\
                  .then_inc(fin_mean_sq.sem, 1)
                dve.wait_ge(*fin_normed.at(0, t + 1))
                nc.vector.tensor_tensor(x_tile[:, t % 2, :], x_norm[:], gain_rows, ALU.mult)\
                  .then_inc(fin_ready.sem, 1)

        @block.gpsimd
        def _(pool):
            steps = [0]

            def step(ins):
                ins.then_inc(pool_step.sem, 1)
                steps[0] += 1
                return steps[0]

            def own(n):
                pool.wait_ge(pool_step.sem, n)

            def inv_sqrt(dst, src, ready):
                nc.gpsimd.tensor_tensor(dst, src, neg_half[:, 0:src.shape[1]], ALU.pow).then_inc(ready.sem, 1)

            nc.gpsimd.memset(eps[:], EPS)
            nc.gpsimd.memset(neg_half[:], -0.5)
            own(step(nc.gpsimd.memset(ident[:], 0.0)))
            nc.gpsimd.affine_select(out=ident[:], in_=ident[:], compare_op=ALU.not_equal, fill=1.0, base=0,
                                    pattern=[[-1, P]], channel_multiplier=1).then_inc(consts_ready.sem, 1)
            nc.gpsimd.memset(ones[:], 1.0).then_inc(consts_ready.sem, 1)
            pool.dma_start(x_res[0:N_CTX, :], x_prompt[0]).then_inc(residual_set.sem, 16)
            pool.dma_start(x_res[N_CTX:N_TOK, :], x_sample[0]).then_inc(residual_set.sem, 16)
            pool.wait_ge(*residual_set.at(0, 2))

            for l in range(DEPTH):
                for t in range(TILES):
                    if t >= 2:
                        pool.wait_ge(*x_norm_ready.at(l, t - 1))
                    pool.dma_start(x_tile[:, t % 2, :], x_res[tokens(t), :]).then_inc(x_loaded[t % 2].sem, 16)
                    if t > 0:
                        pool.wait_ge(*mean_sq_ready.at(l, t))
                        inv_sqrt(rstd[:, 0:1], mean_sq[:, 0:1], rstd_ready)
                pool.wait_ge(*mean_sq_ready.at(l, TILES))
                inv_sqrt(rstd[:, 0:1], mean_sq[:, 0:1], rstd_ready)
                for at in (0, HALO + N_CTX, U_LEN - HALO):
                    last = nc.gpsimd.memset(u[:, :, at:at + HALO], 0.0)
                last.then_inc(halo_zero.sem, 1)
                pool.wait_ge(*x_norm_ready.at(l, TILES))
                for t in range(2):
                    pool.dma_start(x_tile[:, t, :], x_res[tokens(t), :]).then_inc(x_loaded[t].sem, 16)

                def taps(t0, t1):
                    j = CH - 1
                    for t in range(t0, t1):
                        w = conv_cols[:, l, t * CH + j:t * CH + j + 1]
                        src = u[:, j, t:t + C_LEN]
                        if t == 0:
                            own(step(nc.gpsimd.tensor_scalar(acc[:, j, :], src, w,
                                                             par_cols[:, l, C_CB + j:C_CB + j + 1],
                                                             ALU.mult, ALU.add)))
                        else:
                            own(step(nc.gpsimd.tensor_scalar(pool_tmp, src, w, None, ALU.mult)))
                            ins = nc.gpsimd.tensor_tensor(acc[:, j, :], acc[:, j, :], pool_tmp, ALU.add)
                            if t == TAPS - 1:
                                ins.then_inc(conv3_ready.sem, 1)
                            else:
                                own(step(ins))

                def rotate(i):
                    for h in range(H):
                        x = (k_t, q_t)[i][:, h, N_CTX:N_TOK]
                        sw = rope_tmp[:, i * H + h, :]
                        pool.wait_ge(*rope_shuffled.at(l, i * H + h + 1))
                        nc.gpsimd.tensor_tensor(sw, sw, sin_sb[:], ALU.mult)
                        own(step(nc.gpsimd.tensor_tensor(x, x, cos_sb[:], ALU.mult)))
                        nc.gpsimd.tensor_tensor(x, x, sw, ALU.add).then_inc(rope_ready.sem, 1)

                if l == 0:
                    pool.wait_ge(*setup_copied.at(0, 1))
                    pool.wait_ge(*misc_loaded.at(0, 4 * DEPTH + 3 * DEPTH + 2))
                pool.wait_ge(*glu_ready.at(l, CH))
                taps(0, TAPS // 2)
                rotate(0)
                taps(TAPS // 2, TAPS)
                rotate(1)

                def o_inv_sqrt(t):
                    pool.wait_ge(*o_mean_sq_ready.at(l, t + 1))
                    inv_sqrt(o_rstd[:, t % 2, :], o_ss[:, t % 2, :], o_rstd_ready)

                pool.wait_ge(*rope_ready.at(l, 2 * H))
                for s in range(ATT):
                    t, h, b = s // H, s % H, s % 2
                    if s >= 2:
                        pool.wait_ge(*scores_done.at(l, s - 1))
                    for m in range(2):
                        last = nc.gpsimd.tensor_scalar(q_pad[:, b, m, :], q_t[:, h, tokens(t)],
                                                       map_scale[:, m:m + 1], None, ALU.mult)
                    last.then_inc(q_padded.sem, 1)
                    if s > H and s % H == 1:
                        o_inv_sqrt(s // H - 1)
                o_inv_sqrt(TILES - 1)

                for t in range(TILES):
                    if t >= 2:
                        pool.wait_ge(*residual_written[t % 2].at(l, t // 2))
                        pool.wait_ge(*unit_row_ready.at(l, t - 1))
                        pool.dma_start(x_tile[:, t % 2, :], x_res[tokens(t), :]).then_inc(x_loaded[t % 2].sem, 16)
                    pool.wait_ge(*x2_ready.at(l, t + 1))
                    pool.dma_start(x_res[tokens(t), :], x_tile[:, t % 2, :]).then_inc(residual_written[t % 2].sem, 16)
                    pool.wait_ge(*mean_sq2_ready.at(l, t + 1))
                    inv_sqrt(rstd[:, 1:2], mean_sq[:, 1:2], rstd2_ready)

                def gather(e):
                    b = e % 2
                    if e >= 2:
                        pool.wait_ge(*picked_transposed.at(l, e - 1))
                    nc.gpsimd.indirect_dma_start(
                        out=picked[:, b, :], out_offset=None, in_=x_unit,
                        in_offset=bass.IndirectOffsetOnAxis(ap=row_idx[:, e:e + 1], axis=0))\
                      .then_inc(gathered[b].sem, 16)

                pool.wait_ge(*result_taken.at(l, 1))
                pool.wait_ge(*unit_stored.at(l, TILES))
                gather(0)
                gather(1)
                pool.wait_ge(*residual_written[0].at(l, 3))
                pool.wait_ge(*residual_written[1].at(l, 2))
                for e in range(EXPERTS):
                    b = e % 2
                    if e > 0:
                        pool.wait_ge(*residual_written[1 - b].at(l, 2 + b + (e + 1) // 2))
                    pool.wait_ge(*result_taken.at(l, e + 2))
                    nc.gpsimd.indirect_dma_start(
                        out=x_res, out_offset=bass.IndirectOffsetOnAxis(ap=row_idx[:, e:e + 1], axis=0),
                        in_=added[:, b, :], in_offset=None, compute_op=ALU.add)\
                      .then_inc(residual_written[b].sem, 16)
                    if e + 2 < EXPERTS:
                        gather(e + 2)
                pool.wait_ge(*residual_written[1].at(l, 2 + EXPERTS // 2))
                pool.wait_ge(*residual_written[0].at(l, 3 + EXPERTS // 2))

            pool.wait_ge(*unit_used.at(DEPTH - 1, LAYER_UNITS))
            pool.dma_start(h2_t.rearrange("p k n -> p (k n)"),
                           final_norm_g.rearrange("(a n) -> a n", a=1).to_broadcast([P, D])).then_inc(gain_loaded.sem, 16)
            for t in range(TILES):
                b = t % 2
                if t >= 2:
                    pool.wait_ge(*fin_stored[b].at(0, t // 2))
                pool.dma_start(x_tile[:, b, :], x_res[tokens(t), :]).then_inc(fin_loaded[b].sem, 16)
                if t > 0:
                    pool.wait_ge(*fin_mean_sq.at(0, t))
                    inv_sqrt(rstd[:, 2:3], mean_sq[:, 2:3], fin_rstd)
            pool.wait_ge(*fin_mean_sq.at(0, TILES))
            inv_sqrt(rstd[:, 2:3], mean_sq[:, 2:3], fin_rstd)


_INS = ['x_prompt', 'x_sample', 'c', 'cache_k', 'cache_v', 'c_ctx', 'norm1_g', 'w_mod', 'b_mod', 'w_in', 'conv_w',
        'conv_b', 'conv_ln_g', 'conv_ln_b', 'lambda_q1', 'lambda_k1', 'lambda_q2', 'lambda_k2', 'subln_g', 'w_out',
        'norm2_g', 'w_router', 'w_gate', 'w_up', 'w_down', 'final_norm_g']
_OUTS = [((1, N_CTX, D), 'float32'), ((1, N_LAT, D), 'float32'), ((1, DEPTH, N_CTX, H, 2, HD), 'float32'),
         ((1, DEPTH, N_CTX, H, VD), 'float32')]


def rope_constants():
    t = np.arange(N_LAT)
    inv = np.float32(ROPE_BASE) ** (-np.arange(0, ROPE_AXIS, 2, dtype=np.float32) / np.float32(ROPE_AXIS))
    p = np.arange(P)
    pos = np.where((p[:, None] % HD) < ROPE_AXIS, (t // GRID_W)[None, :], (t % GRID_W)[None, :]).astype(np.float32)
    angle = pos * inv[p % (ROPE_AXIS // 2)][:, None].astype(np.float32)
    sign = np.where(p % ROPE_AXIS < ROPE_AXIS // 2, -1.0, 1.0).astype(np.float32)
    return np.cos(angle).astype(np.float32), (np.sin(angle) * sign[:, None]).astype(np.float32)


def kernel(**inputs):
    import numpy as _np
    import concourse.bacc as _bacc
    from concourse import mybir as _mybir
    from concourse.bass_utils import run_bass_kernel_spmd as _run

    nc = _bacc.Bacc("TRN2", target_bir_lowering=False, num_devices=1)
    given = {name: _np.ascontiguousarray(inputs[name]) for name in _INS}
    given["rope_cos"], given["rope_sin"] = rope_constants()
    arrays, args = {}, []
    for name, a in given.items():
        arrays[f"in_{name}_dram"] = a
        args.append(nc.dram_tensor(f"in_{name}_dram", a.shape, _mybir.dt.from_np(a.dtype), kind="ExternalInput").ap())
    for i, (shape, dtype) in enumerate(_OUTS):
        dt = _mybir.dt.from_np(_np.dtype(dtype))
        args.append(nc.dram_tensor(f"out_{i}_dram", shape, dt, kind="ExternalOutput").ap())
    build(nc, *args)
    r = _run(nc, [arrays], core_ids=[0])
    return tuple(r.results[0][f"out_{i}_dram"] for i in range(len(_OUTS)))
```

```python
import math
from contextlib import ExitStack

import numpy as np
import concourse.bass as bass
from concourse import mybir

D = 1024
DEPTH = 2
N_CTX, N_LAT, PAST = 128, 512, 128
N_TOK = N_CTX + N_LAT
H, HD = 4, 64
VD = 2 * HD
D_CONV, TAPS = 512, 31
GRID_W = 64
ROPE_BASE, ROPE_AXIS = 10000.0, HD // 2
EXPERTS, D_EXP = 16, 1024
CAP_CTX, CAP_LAT = 2 * N_CTX // EXPERTS, 2 * N_LAT // EXPERTS
CAP = CAP_LAT + CAP_CTX
EPS = 1e-6

P = 128
KD = D // P
TILES = N_TOK // P
CH = D_CONV // P
HALO = TAPS // 2
U_LEN = HALO + N_CTX + HALO + N_LAT + HALO
C_LEN = N_CTX + HALO + N_LAT
LAT0 = N_CTX + HALO
BANK = 512
UNIT = KD * BANK
SLOTS = 6
DENSE_SLOTS = 4
MOD_UNITS = 6 * D // BANK
PROJ_UNITS = (2 * D_CONV + 4 * H * HD + H * VD) // BANK
OUT_UNITS = 2
DENSE_UNITS = MOD_UNITS + PROJ_UNITS + OUT_UNITS
LAYER_UNITS = DENSE_UNITS + 6 * EXPERTS
CAP_W = 96
MOD_ORDER = (0, 1, 2, 3, 4, 5, 10, 11, 6, 7, 8, 9)
MOD_FIRST = 4
D_PROJ = MOD_FIRST
D_MOD2 = D_PROJ + PROJ_UNITS
D_OUT = D_MOD2 + MOD_UNITS - MOD_FIRST
BLK = BANK // P
ATT = TILES * H
OUT_TILES = (1, 2, 3, 4, 0)
C_BMOD, C_N1, C_N2, C_CB, C_LG, C_LB, C_SUB, C_ALL = 0, 48, 56, 64, 68, 72, 76, 77


class Signal:

    def __init__(self, sem, per_layer, unit=1):
        self.sem, self.per_layer, self.unit = sem, per_layer, unit

    def at(self, layer, n):
        return self.sem, (n + layer * self.per_layer) * self.unit


def build(nc, x_prompt, x_sample, c, cache_k, cache_v, c_ctx, norm1_g, w_mod, b_mod, w_in, conv_w, conv_b,
          conv_ln_g, conv_ln_b, lambda_q1, lambda_k1, lambda_q2, lambda_k2, subln_g, w_out, norm2_g,
          w_router, w_gate, w_up, w_down, final_norm_g, rope_cos, rope_sin,
          y_prompt, y_sample, new_cache_k, new_cache_v):
    f32, u32 = mybir.dt.float32, mybir.dt.uint32
    ALU, ACT = mybir.AluOpType, mybir.ActivationFunctionType
    AX = mybir.AxisListType.X
    lam_init = [0.8 - 0.6 * math.exp(-0.3 * l) for l in range(DEPTH)]

    ctx = ExitStack()
    with ctx:
        def sb(name, shape, dt=f32):
            return ctx.enter_context(nc.sbuf_tensor(name, shape, dt))

        def signal(name, per_layer=0, unit=1):
            return Signal(ctx.enter_context(nc.semaphore(name)), per_layer, unit)

        x_res = nc.dram_tensor("x_res", (N_TOK, D), f32, kind="Internal").ap()
        x_unit = nc.dram_tensor("x_unit", (N_TOK, D), f32, kind="Internal").ap()

        ring = sb("weight_ring", [P, SLOTS, UNIT])
        free_slots = ring[:, DENSE_SLOTS:SLOTS, :].rearrange("p s n -> p (s n)")
        mix = sb("mix", [P, KD, N_TOK])
        u_gate = sb("u_gate", [P, CH * U_LEN])
        u = u_gate[:, :].rearrange("p (c n) -> p c n", c=CH)
        gate1 = u_gate[:, 0:2 * D].rearrange("p (v n) -> p v n", v=2)
        qk = sb("qk", [P, 2, H, N_TOK])
        q_t, k_t = qk[:, 0], qk[:, 1]
        qk_flat = qk[:, :, :, :].rearrange("p a h n -> p (a h n)")
        picked = qk_flat[0:CAP, 0:2 * D].rearrange("p (b n) -> p b n", b=2)
        added = qk_flat[0:CAP, 2 * D:4 * D].rearrange("p (b n) -> p b n", b=2)
        v_sb = sb("v_sb", [P, TILES * BANK])
        v_tok = v_sb[:, :].rearrange("p (t n) -> p t n", t=TILES)
        h2_t = v_sb[:, 0:D].rearrange("p (k n) -> p k n", k=KD)
        picked_t = v_sb[:, D:D + 2 * KD * CAP_W].rearrange("p (b k n) -> p b k n", b=2, k=KD)
        x_all = qk_flat.rearrange("p (t n) -> p t n", t=TILES)
        mix_flat = mix[:, :, :].rearrange("p k n -> p (k n)")
        hid = mix_flat[:, 0:KD * CAP].rearrange("p (k n) -> p k n", k=KD)
        silu_g = mix_flat[:, KD * CAP:2 * KD * CAP].rearrange("p (b n) -> p b n", b=2)
        x_tile = sb("x_tile", [P, 2, D])
        x_norm = sb("x_norm", [P, D])
        conv_tmp = sb("conv_tmp", [P, 2, C_LEN])
        key_rows = conv_tmp[:, 0, 0:BANK]
        acc = free_slots[:, 0:CH * C_LEN].rearrange("p (c n) -> p c n", c=CH)
        o = CH * C_LEN
        rope_tmp = free_slots[:, o:o + 2 * H * N_LAT].rearrange("p (b n) -> p b n", b=2 * H)
        prob = free_slots[:, o:o + 4 * N_TOK].rearrange("p (b c n) -> p b c n", b=2, c=2)
        a_row = free_slots[:, o + 4 * N_TOK:o + 6 * N_TOK].rearrange("p (b n) -> p b n", b=2)
        a_col = free_slots[:, o + 6 * N_TOK:o + 7 * N_TOK]
        conv_rstd = rope_tmp[:, 0:2, :].rearrange("p b n -> p (b n)")[:, 0:C_LEN]
        gate1_cols = free_slots[:, 0:2 * D].rearrange("p (v k n) -> p v k n", v=2, k=KD)
        gate2_cols = free_slots[:, o + 7 * N_TOK:o + 7 * N_TOK + KD * CAP].rearrange("p (k n) -> p k n", k=KD)
        assert o + 7 * N_TOK + KD * CAP <= 2 * UNIT and 2 * D <= o
        o_tok = sb("o_tok", [P, 2, H, VD])
        o_sq = conv_tmp[:, 1, 0:BANK].rearrange("p (h n) -> p h n", h=H)
        q_pad = sb("q_pad", [P, 2, 2, P])
        map_scale = sb("map_scale", [P, 2])
        cos_sb = sb("cos_sb", [P, N_LAT])
        sin_sb = sb("sin_sb", [P, N_LAT])
        past_k_t = sb("past_k_t", [P, DEPTH, H, PAST])
        past_v = sb("past_v", [P, DEPTH, H * VD])
        gate2 = sb("gate2", [CAP, D])
        scale2_x = sb("scale2_x", [P, KD, CAP])
        shift2_x = sb("shift2_x", [P, KD, CAP])
        ident = sb("ident", [P, P])
        ones = sb("ones", [P, P])
        conv_cols = sb("conv_cols", [P, DEPTH, TAPS * CH])
        par_cols = sb("par_cols", [P, DEPTH, C_ALL])
        cond_rows = free_slots[0:2 * KD, 0:P]
        conv_rows = free_slots[0:TAPS * CH, P:P + DEPTH * P].rearrange("p (l n) -> p l n", l=DEPTH)
        par_rows = free_slots[0:C_ALL, 3 * P:3 * P + DEPTH * P].rearrange("p (l n) -> p l n", l=DEPTH)
        past_k = free_slots[:, 5 * P:5 * P + DEPTH * BANK].rearrange("p (l n) -> p l n", l=DEPTH)
        o = 5 * P + DEPTH * BANK
        lam_rows = free_slots[:, o:o + DEPTH * 4 * HD].rearrange("p (l f n) -> p l f n", l=DEPTH, f=4)
        o += DEPTH * 4 * HD
        lam_prod = free_slots[:, o:o + DEPTH * 2 * HD].rearrange("p (l f n) -> p l f n", l=DEPTH, f=2)
        cond_silu = sb("cond_silu", [P, KD, 2])
        lam_e = sb("lam_e", [P, DEPTH, 2])
        neg_lam = sb("neg_lam", [P, DEPTH])
        sub_cols = sb("sub_cols", [P, DEPTH])
        router = sb("router", [P, DEPTH, KD, EXPERTS])
        mod = sb("mod", [P, 6 * KD, 2])
        scale1 = sb("scale1", [P, KD, 2])
        scale2 = sb("scale2", [P, KD, 2])
        ssq = sb("ssq", [P, TILES + 1])
        mean_sq = sb("mean_sq", [P, TILES + 1])
        rstd = sb("rstd", [P, TILES + 1])
        neg_half = sb("neg_half", [P, TILES])
        eps = sb("eps", [P, 1])
        neg_max = sb("neg_max", [P, 2, 2, 2])
        neg_m = sb("neg_m", [P, 2, 2])
        row_sum = sb("row_sum", [P, 2, 2, 2])
        row_r = sb("row_r", [P, 2, 2])
        row_c = sb("row_c", [P, 2])
        o_ss = sb("o_ss", [P, 2, H])
        o_rstd = sb("o_rstd", [P, 2, H])
        r_max = sb("r_max", [P, 1])
        r_sum = sb("r_sum", [P, 1])
        r_exp = sb("r_exp", [P, EXPERTS])
        aff = sb("aff", [P, EXPERTS])
        pick_space = qk_flat[0:EXPERTS, 4 * D:4 * D + N_TOK + 3 * CAP]
        aff_t = pick_space[:, 0:N_TOK]
        top_v = pick_space[:, N_TOK:N_TOK + CAP]
        top_f = pick_space[:, N_TOK + CAP:N_TOK + 2 * CAP]
        top_i = pick_space[:, N_TOK + 2 * CAP:N_TOK + 3 * CAP].bitcast(u32)
        row_idx = sb("row_idx", [CAP, EXPERTS], u32)
        gsel = sb("gsel", [CAP, EXPERTS])
        ps = ctx.enter_context(nc.psum_tensor("ps", [P, 8, BANK], f32))

        consts_ready = signal("consts_ready")
        cond_loaded = signal("cond_loaded", unit=16)
        rows_loaded = signal("rows_loaded", unit=16)
        misc_loaded = signal("misc_loaded", unit=16)
        setup_transposed = signal("setup_transposed")
        setup_copied = signal("setup_copied")
        cond_ready = signal("cond_ready")
        lam_summed = signal("lam_summed")
        lam_exped = signal("lam_exped")
        lam_ready = signal("lam_ready")
        slot_dense = [len(range(s, DENSE_UNITS, DENSE_SLOTS)) if s < DENSE_SLOTS else 0 for s in range(SLOTS)]
        slot_loaded = [signal(f"slot{s}_loaded", slot_dense[s] + EXPERTS, 16) for s in range(SLOTS)]
        unit_used = signal("unit_used", LAYER_UNITS)
        mod1_ready = signal("mod1_ready", 1)
        mod2_ready = signal("mod2_ready", 1)
        tile_loaded = [signal(f"tile_loaded{t}", 1, 16) for t in range(TILES)]
        x_loaded = [signal(f"x_loaded{b}", 3 - b, 16) for b in range(2)]
        ssq_ready = signal("ssq_ready", 1)
        mean_sq_ready = signal("mean_sq_ready", 1)
        rstd_ready = signal("rstd_ready", 1)
        x_norm_ready = signal("x_norm_ready", TILES)
        x_transposed = signal("x_transposed", TILES)
        h_lo_ready = signal("h_lo_ready", TILES)
        h_hi_ready = signal("h_hi_ready", TILES)
        halo_zero = signal("halo_zero", 1)
        proj_done = signal("proj_done", 4 * (BLK - 1) + TILES - 1)
        proj_copied = signal("proj_copied", 4 * BLK + TILES)
        glu_ready = signal("glu_ready", CH)
        rope_shuffled = signal("rope_shuffled", 2 * H)
        rope_ready = signal("rope_ready", 2 * H)
        conv_ready = signal("conv_ready", CH)
        keys_transposed = signal("keys_transposed", 1)
        keys_copied = signal("keys_copied", 1)
        cache_stored = signal("cache_stored", 2, 16)
        mean_ready = signal("mean_ready", 1)
        centred = signal("centred", CH)
        squared = signal("squared", CH)
        square_used = signal("square_used", CH)
        conv_std_ready = signal("conv_std_ready", 1)
        conv_normed = signal("conv_normed", CH)
        conv_out_ready = signal("conv_out_ready", 1)
        gate_cols_ready = signal("gate_cols_ready", 1)
        gates_transposed = signal("gates_transposed", 2)
        gates_ready = signal("gates_ready", 2)
        q_padded = signal("q_padded", ATT)
        scores_done = signal("scores_done", ATT)
        neg_m_ready = signal("neg_m_ready", ATT)
        probs_ready = signal("probs_ready", ATT)
        a_ready = signal("a_ready", ATT)
        a_transposed = signal("a_transposed", ATT)
        a_col_ready = signal("a_col_ready", ATT)
        pv_done = signal("pv_done", ATT)
        o_copied = signal("o_copied", ATT)
        o_mean_sq_ready = signal("o_mean_sq_ready", TILES)
        o_rstd_ready = signal("o_rstd_ready", TILES)
        o_normed = signal("o_normed", TILES)
        o_transposed = signal("o_transposed", TILES)
        o_mixed = signal("o_mixed", TILES)
        out_done = signal("out_done", TILES - 1)
        x2_ready = signal("x2_ready", TILES)
        ssq2_ready = signal("ssq2_ready", TILES)
        mean_sq2_ready = signal("mean_sq2_ready", TILES)
        rstd2_ready = signal("rstd2_ready", TILES)
        residual_written = [signal(f"residual_written{b}", 3 - b + EXPERTS // 2, 16) for b in range(2)]
        unit_row_ready = signal("unit_row_ready", TILES)
        unit_stored = signal("unit_stored", TILES, 16)
        x2_transposed = signal("x2_transposed", TILES)
        h2_lo_ready = signal("h2_lo_ready", TILES)
        h2_hi_ready = signal("h2_hi_ready", TILES)
        logits_done = signal("logits_done", TILES)
        r_max_ready = signal("r_max_ready", TILES)
        r_exp_ready = signal("r_exp_ready", TILES)
        aff_ready = signal("aff_ready", TILES)
        aff_transposed = signal("aff_transposed", TILES)
        padding_zero = signal("padding_zero", 1)
        aff_copied = signal("aff_copied", TILES)
        top_ready = signal("top_ready", 1)
        top_transposed = signal("top_transposed", 1)
        result_taken = signal("result_taken", 1 + EXPERTS)
        gathered = [signal(f"gathered{b}", EXPERTS // 2, 16) for b in range(2)]
        picked_transposed = signal("picked_transposed", EXPERTS)
        picked_scaled = signal("picked_scaled", EXPERTS)
        picked_ready = signal("picked_ready", EXPERTS)
        silu_ready = signal("silu_ready", 2 * EXPERTS)
        hid_ready = signal("hid_ready", 2 * EXPERTS)
        gain_loaded = signal("gain_loaded", unit=16)
        y_ready = signal("y_ready")
        y_stored = signal("y_stored", unit=16)
        dve_step = signal("dve_step")
        pool_step = signal("pool_step")

        block = ctx.enter_context(nc.Block())

        def halves(bank):
            return ps[:, bank, 0:BLK * CAP_W].rearrange("p (f n) -> p f n", f=BLK)[:, :, 0:CAP]

        def tokens(t):
            return slice(t * P, (t + 1) * P)

        def vec(t):
            return 0 if t == 0 else 1

        def input_rows(t):
            return x_prompt[0] if t == 0 else x_sample[0, (t - 1) * P:t * P, :]

        @block.sync
        def _(sp):
            def dense_unit(l, d, src):
                slot, k = d % DENSE_SLOTS, d // DENSE_SLOTS
                if d >= DENSE_SLOTS:
                    sp.wait_ge(*unit_used.at(l, d - DENSE_SLOTS + 1))
                elif l > 0:
                    sp.wait_ge(*unit_used.at(l - 1, DENSE_UNITS + 6 * (EXPERTS - 1) + d + 1))
                sp.dma_start(ring[:, slot, :].rearrange("p (k n) -> p k n", k=KD), src)\
                  .then_inc(slot_loaded[slot].sem, 16)

            def expert_src(l, e, i):
                if i < 4:
                    w = (w_gate, w_up)[i % 2]
                    return w[l, e].rearrange("(k p) n -> p k n", p=P)[:, :, (i // 2) * BANK:(i // 2 + 1) * BANK]
                return w_down[l, e].rearrange("(k p) n -> p k n", p=P)[:, (i - 4) * 4:(i - 3) * 4, :]

            def expert_unit(l, e, i):
                kk = KD if i < 4 else KD // 2
                sp.dma_start(ring[:, i, :].rearrange("p (k n) -> p k n", k=kk), expert_src(l, e, i))\
                  .then_inc(slot_loaded[i].sem, 16)

            sp.dma_start(cond_rows[0:KD, :], c_ctx.rearrange("(k p) -> k p", p=P)).then_inc(cond_loaded.sem, 16)
            sp.dma_start(cond_rows[KD:2 * KD, :], c[0].rearrange("(k p) -> k p", p=P)).then_inc(cond_loaded.sem, 16)
            for l in range(DEPTH):
                cols = w_mod[l].rearrange("(k p) n -> p k n", p=P)
                proj = w_in[l].rearrange("(k p) n -> p k n", p=P)
                outw = w_out[l].rearrange("(k p) n -> p k n", p=P)
                order = [(cols, m) for m in MOD_ORDER[:MOD_FIRST]]
                order += [(proj, m) for m in (0, 1, 3, 2, 4)]
                order += [(cols, m) for m in MOD_ORDER[MOD_FIRST:]]
                for d, (src, m) in enumerate(order):
                    dense_unit(l, d, src[:, :, m * BANK:(m + 1) * BANK])
                for half in range(OUT_UNITS):
                    d = D_OUT + half
                    sp.wait_ge(*unit_used.at(l, d - DENSE_SLOTS + 1))
                    sp.dma_start(ring[:, d % DENSE_SLOTS, :].rearrange("p (k n) -> p k n", k=KD // 2),
                                 outw[:, half * 4:half * 4 + 4, :]).then_inc(slot_loaded[d % DENSE_SLOTS].sem, 16)
                for i in (0, 3, 4, 5, 1, 2):
                    if i in (0, 3):
                        sp.wait_ge(*unit_used.at(l, D_OUT - (1 if i == 0 else 2) + 1))
                    elif i == 4:
                        sp.wait_ge(*pv_done.at(l, ATT))
                        sp.wait_ge(*gates_transposed.at(l, 2))
                    elif i in (1, 2):
                        sp.wait_ge(*unit_used.at(l, D_OUT + i))
                    expert_unit(l, 0, i)
                with sp.Fori(1, EXPERTS) as e:
                    for i in range(6):
                        sp.wait_ge(*unit_used.at(l, e * 6 + (DENSE_UNITS - 6 + i + 1)))
                        expert_unit(l, e, i)

        @block.tensor
        def _(pe):
            pe.wait_ge(*consts_ready.at(0, 2))
            pe.wait_ge(*cond_loaded.at(0, 2))
            nc.tensor.transpose(ps[:, 0, 0:2 * KD], cond_rows, ident[0:2 * KD, 0:2 * KD])\
              .then_inc(setup_transposed.sem, 1)
            def setup_transposes():
                pe.wait_ge(*rows_loaded.at(0, 8 * DEPTH))
                for l in range(DEPTH):
                    nc.tensor.transpose(ps[:, 1, l * TAPS * CH:(l + 1) * TAPS * CH], conv_rows[:, l, :],
                                        ident[0:TAPS * CH, 0:TAPS * CH])
                    o = DEPTH * TAPS * CH + l * C_ALL
                    last = nc.tensor.transpose(ps[:, 1, o:o + C_ALL], par_rows[:, l, :], ident[0:C_ALL, 0:C_ALL])
                last.then_inc(setup_transposed.sem, 1)
                pe.wait_ge(*misc_loaded.at(0, 4 * DEPTH + 3 * DEPTH + 2))
                for l in range(DEPTH):
                    for h in range(H):
                        last = nc.tensor.transpose(ps[:, 2 + l, tokens(h)], past_k[:, l, tokens(h)], ident[:])
                last.then_inc(setup_transposed.sem, 1)
                pe.wait_ge(*setup_copied.at(0, 1))

            pe.wait_ge(*cond_ready.at(0, 1))

            def wait_unit(l, d):
                pe.wait_ge(*slot_loaded[d % DENSE_SLOTS].at(l, d // DENSE_SLOTS + 1))

            def modulate(l, d, at, bank):
                wait_unit(l, d)
                w = ring[:, d % DENSE_SLOTS, :].rearrange("p (k n) -> p k n", k=KD)
                for b in range(BLK):
                    col = 2 * (at * BLK + b)
                    for k in range(KD):
                        last = nc.tensor.matmul(ps[:, bank, col:col + CAP_W], w[:, k, tokens(b)],
                                                cond_silu[:, k, :].unsqueeze(1).to_broadcast([P, CAP_W // 2, 2]),
                                                start=(k == 0), stop=(k == KD - 1))
                last.then_inc(unit_used.sem, 1)

            for l in range(DEPTH):
                for m in range(MOD_FIRST):
                    modulate(l, m, m, 7)
                if l == 0:
                    setup_transposes()

                for t in range(TILES):
                    pe.wait_ge(*x_norm_ready.at(l, t + 1))
                    if t >= 3:
                        pe.wait_ge(*h_lo_ready.at(l, t - 2))
                        pe.wait_ge(*h_hi_ready.at(l, t - 2))
                    for k in range(KD):
                        last = nc.tensor.transpose(ps[:, 2 * (t % 3) + k // 4, tokens(k % 4)],
                                                   x_all[:, t, tokens(k)], ident[:])
                    last.then_inc(x_transposed.sem, 1)

                pe.wait_ge(*h_lo_ready.at(l, TILES))
                pe.wait_ge(*h_hi_ready.at(l, TILES))
                for i in range(4):
                    d = D_PROJ + i
                    wait_unit(l, d)
                    w = ring[:, d % DENSE_SLOTS, :].rearrange("p (k n) -> p k n", k=KD)
                    for b in range(BLK):
                        n = i * BLK + b
                        if n >= 3:
                            pe.wait_ge(*proj_copied.at(l, n - 2))
                        for bank, cols in ((0, slice(N_CTX, N_TOK)), (1, slice(0, N_CTX))):
                            for k in range(KD):
                                last = nc.tensor.matmul(
                                    ps[:, 2 * (n % 3) + bank, 0:cols.stop - cols.start], w[:, k, tokens(b)],
                                    mix[:, k, cols], start=(k == 0), stop=(k == KD - 1))
                        last.then_inc((unit_used if b == BLK - 1 else proj_done).sem, 1)
                d = D_PROJ + 4
                wait_unit(l, d)
                w = ring[:, d % DENSE_SLOTS, :].rearrange("p (k n) -> p k n", k=KD)
                for t in range(TILES):
                    n = 4 * BLK + t
                    pe.wait_ge(*proj_copied.at(l, n - 2))
                    for k in range(KD):
                        last = nc.tensor.matmul(ps[:, 2 * (n % 3), :], mix[:, k, tokens(t)], w[:, k, :],
                                                start=(k == 0), stop=(k == KD - 1))
                    last.then_inc((unit_used if t == TILES - 1 else proj_done).sem, 1)

                for h in range(H):
                    last = nc.tensor.transpose(ps[:, 6, tokens(h)], k_t[:, h, 0:N_CTX], ident[:])
                last.then_inc(keys_transposed.sem, 1)

                pe.wait_ge(*mod1_ready.at(l, 1))
                for i in range(4):
                    modulate(l, D_MOD2 + i, i, 7)

                pe.wait_ge(*proj_copied.at(l, 4 * BLK + TILES))
                pe.wait_ge(*conv_ready.at(l, CH))
                for c0, c1, bank in ((0, BANK, 0), (BANK, C_LEN, 1)):
                    for j in range(CH):
                        last = nc.tensor.matmul(ps[:, bank, 0:c1 - c0], ones[:], acc[:, j, c0:c1],
                                                start=(j == 0), stop=(j == CH - 1))
                last.then_inc(mean_ready.sem, 1)
                pe.wait_ge(*keys_copied.at(l, 1))
                for i in range(2):
                    modulate(l, D_MOD2 + 4 + i, i, 6)
                for j in range(CH):
                    pe.wait_ge(*squared.at(l, j + 1))
                    for c0, c1, bank in ((0, BANK, 2), (BANK, C_LEN, 3)):
                        last = nc.tensor.matmul(ps[:, bank, 0:c1 - c0], ones[:], conv_tmp[:, j % 2, c0:c1],
                                                start=(j == 0), stop=(j == CH - 1))
                    last.then_inc(square_used.sem, 1)
                for i in range(2, 4):
                    modulate(l, D_MOD2 + 4 + i, i, 6)

                def scores(s):
                    t, h = s // H, s % H
                    b0 = 3 * (s % 2)
                    pe.wait_ge(*q_padded.at(l, s + 1))
                    if s >= 2:
                        pe.wait_ge(*probs_ready.at(l, s - 1))
                    for m in range(2):
                        q = q_pad[:, s % 2, m, :]
                        if t > 0:
                            nc.tensor.matmul(ps[:, b0 + m, :], q, k_t[:, h, N_CTX:N_TOK], start=True, stop=True)
                        keys = past_k_t[:, l, h, :] if t > 0 else k_t[:, h, 0:N_CTX]
                        last = nc.tensor.matmul(ps[:, b0 + 2, tokens(m)], q, keys, start=True, stop=True)
                    last.then_inc(scores_done.sem, 1)

                def o_transposes(t):
                    pe.wait_ge(*o_normed.at(l, t + 1))
                    for h in range(H):
                        last = nc.tensor.transpose(ps[:, 6, tokens(h)], o_tok[:, t % 2, h, :], ident[:])
                    last.then_inc(o_transposed.sem, 1)

                pe.wait_ge(*conv_std_ready.at(l, 1))
                pe.wait_ge(*mod2_ready.at(l, 1))
                scores(0)
                scores(1)
                for s in range(ATT):
                    t, h = s // H, s % H
                    pe.wait_ge(*a_ready.at(l, s + 1))
                    if s > 0:
                        pe.wait_ge(*o_copied.at(l, s))
                    if t > 0 and h == 2:
                        pe.wait_ge(*o_mixed.at(l, t))
                    tiles = range(1) if t == 0 else range(TILES)
                    for j in tiles:
                        dst = ps[:, 6, tokens(j)] if j < 4 else ps[:, 7, 0:P]
                        last = nc.tensor.transpose(dst, a_row[:, s % 2, tokens(j)], ident[:])
                    last.then_inc(a_transposed.sem, 1)
                    if s + 2 < ATT:
                        scores(s + 2)
                    pe.wait_ge(*a_col_ready.at(l, s + 1))
                    for j in tiles:
                        if t == 0:
                            vals = v_tok[:, 0, tokens(h)]
                        else:
                            vals = v_tok[:, j + 1, tokens(h)] if j < 4 else past_v[:, l, tokens(h)]
                        last = nc.tensor.matmul(ps[:, 7, 2 * P:3 * P], a_col[:, tokens(j)], vals,
                                                start=(j == 0), stop=(j == len(tiles) - 1))
                    last.then_inc(pv_done.sem, 1)
                    if t > 0 and h == 1:
                        o_transposes(t - 1)
                pe.wait_ge(*gate_cols_ready.at(l, 1))
                for v in range(2):
                    for k in range(KD):
                        last = nc.tensor.transpose(ps[:, 2 + 2 * v + k // 4, tokens(k % 4)], gate1_cols[:, v, k, :],
                                                   ident[:])
                last.then_inc(gates_transposed.sem, 1)
                o_transposes(TILES - 1)

                def out_tile(i, k0, k1):
                    t = OUT_TILES[i]
                    if i >= 2 and k0 == 0:
                        pe.wait_ge(*x2_ready.at(l, i - 1))
                    for k in range(k0, k1):
                        d = D_OUT + k // 4
                        if i == 0 and k % 4 == 0:
                            wait_unit(l, d)
                        w = ring[:, d % DENSE_SLOTS, :].rearrange("p (k n) -> p k n", k=KD // 2)
                        for n in range(2):
                            last = nc.tensor.matmul(ps[:, 2 * (i % 2) + n, :], mix[:, k, tokens(t)],
                                                    w[:, k % 4, n * BANK:(n + 1) * BANK],
                                                    start=(k == 0), stop=(k == KD - 1))
                        if i == TILES - 1 and k == 3:
                            last.then_inc(unit_used.sem, 1)
                    if k1 == KD:
                        last.then_inc((unit_used if i == TILES - 1 else out_done).sem, 1)

                def x2_transposes(i):
                    pe.wait_ge(*unit_row_ready.at(l, i + 1))
                    for k in range(KD):
                        last = nc.tensor.transpose(ps[:, 4 + k // 4, tokens(k % 4)], x_norm[:, tokens(k)], ident[:])
                    last.then_inc(x2_transposed.sem, 1)

                def logits(i):
                    pe.wait_ge(*h2_lo_ready.at(l, i + 1))
                    pe.wait_ge(*h2_hi_ready.at(l, i + 1))
                    if i > 0:
                        pe.wait_ge(*r_exp_ready.at(l, i))
                    for k in range(KD):
                        last = nc.tensor.matmul(ps[:, 6, 0:EXPERTS], h2_t[:, k, :], router[:, l, k, :],
                                                start=(k == 0), stop=(k == KD - 1))
                    last.then_inc(logits_done.sem, 1)

                def aff_transpose(i):
                    pe.wait_ge(*aff_ready.at(l, i + 1))
                    if i > 0:
                        pe.wait_ge(*aff_copied.at(l, i))
                    nc.tensor.transpose(ps[0:EXPERTS, 7, 0:P], aff[:], ident[:]).then_inc(aff_transposed.sem, 1)

                pe.wait_ge(*conv_out_ready.at(l, 1))
                pe.wait_ge(*o_mixed.at(l, TILES))
                out_tile(0, 0, KD)
                pe.wait_ge(*gates_ready.at(l, 1))
                for k in range(KD):
                    last = nc.tensor.transpose(ps[0:CAP, 4 + k // 4, tokens(k % 4)], gate2_cols[:, k, :], ident[:])
                last.then_inc(gates_transposed.sem, 1)
                out_tile(1, 0, KD)
                pe.wait_ge(*gates_ready.at(l, 2))
                x2_transposes(0)
                out_tile(2, 0, KD)
                logits(0)
                x2_transposes(1)
                out_tile(3, 0, KD)
                logits(1)
                aff_transpose(0)
                x2_transposes(2)
                out_tile(4, 0, 4)
                logits(2)
                aff_transpose(1)
                x2_transposes(3)
                out_tile(4, 4, 6)
                logits(3)
                aff_transpose(2)
                out_tile(4, 6, 7)
                aff_transpose(3)
                out_tile(4, 7, KD)
                x2_transposes(4)
                logits(4)
                aff_transpose(4)

                pe.wait_ge(*top_ready.at(l, 1))
                nc.tensor.transpose(ps[0:CAP, 4, 0:EXPERTS], top_f, ident[0:EXPERTS, 0:EXPERTS])
                nc.tensor.transpose(ps[0:CAP, 5, 0:EXPERTS], top_v, ident[0:EXPERTS, 0:EXPERTS])\
                  .then_inc(top_transposed.sem, 1)
                pe.wait_ge(*result_taken.at(l, 1))

                def picked_transposes(e, b, rnd):
                    pe.wait_ge(*gathered[b].at(l, rnd + 1))
                    for k in range(KD):
                        last = nc.tensor.transpose(ps[:, 6 + k // 4, (k % 4) * CAP:(k % 4 + 1) * CAP],
                                                   picked[:, b, tokens(k)], ident[0:CAP, 0:CAP])
                    last.then_inc(picked_transposed.sem, 1)

                def gate_up(e, b):
                    pe.wait_ge(*picked_ready.at(l, e + 1))
                    for i in range(4):
                        pe.wait_ge(*slot_loaded[i].at(l, e + (slot_dense[i] + 1)))
                        w = ring[:, i, :].rearrange("p (k n) -> p k n", k=KD)
                        for f in range(BLK):
                            for k in range(KD):
                                last = nc.tensor.matmul(ps[:, i, f * CAP_W:(f + 1) * CAP_W], w[:, k, tokens(f)],
                                                        picked_t[:, b, k, :], start=(k == 0), stop=(k == KD - 1))
                        last.then_inc(unit_used.sem, 1)

                def down(e):
                    pe.wait_ge(*result_taken.at(l, e + 1))
                    for half in range(2):
                        pe.wait_ge(*slot_loaded[4 + half].at(l, e + 1))
                        pe.wait_ge(*hid_ready.at(l, 2 * e + half + 1))
                        w = ring[:, 4 + half, :].rearrange("p (k n) -> p k n", k=KD // 2)
                        for kk in range(KD // 2):
                            k = half * (KD // 2) + kk
                            for n in range(2):
                                last = nc.tensor.matmul(ps[0:CAP, 4 + n, :], hid[:, k, :],
                                                        w[:, kk, n * BANK:(n + 1) * BANK],
                                                        start=(k == 0), stop=(k == KD - 1))
                        last.then_inc(unit_used.sem, 1)

                pe.wait_ge(*padding_zero.at(l, 1))
                with pe.Fori(0, EXPERTS // 2) as r:
                    picked_transposes(r * 2, 0, r)
                    gate_up(r * 2, 0)
                    picked_transposes(r * 2 + 1, 1, r)
                    down(r * 2)
                    gate_up(r * 2 + 1, 1)
                    down(r * 2 + 1)

        @block.scalar
        def _(act):
            for l in range(DEPTH):
                act.dma_start(conv_rows[:, l, :], conv_w[l].rearrange("t (k p) -> (t k) p", p=P))\
                   .then_inc(rows_loaded.sem, 16)
                for src, at in ((b_mod, C_BMOD), (norm1_g, C_N1), (norm2_g, C_N2), (conv_b, C_CB),
                                (conv_ln_g, C_LG), (conv_ln_b, C_LB), (subln_g, C_SUB)):
                    n = src.shape[1] // P
                    act.dma_start(par_rows[at:at + n, l, :], src[l].rearrange("(k p) -> k p", p=P))\
                       .then_inc(rows_loaded.sem, 16)
            for l in range(DEPTH):
                for f, src in enumerate((lambda_q1, lambda_k1, lambda_q2, lambda_k2)):
                    act.dma_start(lam_rows[:, l, f, :], src[l:l + 1, :].to_broadcast([P, HD]))\
                       .then_inc(misc_loaded.sem, 16)
                act.dma_start(past_k[:, l, :], cache_k[0, l].rearrange("t h c d -> t (h c d)"))\
                   .then_inc(misc_loaded.sem, 16)
                act.dma_start(past_v[:, l, :], cache_v[0, l].rearrange("t h d -> t (h d)"))\
                   .then_inc(misc_loaded.sem, 16)
                act.dma_start(router[:, l], w_router[l].rearrange("(k p) e -> p k e", p=P))\
                   .then_inc(misc_loaded.sem, 16)
            act.dma_start(cos_sb[:], rope_cos).then_inc(misc_loaded.sem, 16)
            act.dma_start(sin_sb[:], rope_sin).then_inc(misc_loaded.sem, 16)

            act.wait_ge(*setup_transposed.at(0, 1))
            nc.scalar.activation(cond_silu[:].rearrange("p k v -> p v k"),
                                 ps[:, 0, 0:2 * KD].rearrange("p (v k) -> p v k", v=2), ACT.Silu)\
              .then_inc(cond_ready.sem, 1)

            for l in range(DEPTH):
                def h_hi(t):
                    act.wait_ge(*x_transposed.at(l, t + 1))
                    if t == 0:
                        act.wait_ge(*mod1_ready.at(l, 1))
                    for k in range(4, KD):
                        last = nc.scalar.activation(mix[:, k, tokens(t)], ps[:, 2 * (t % 3) + 1, tokens(k - 4)],
                                                    ACT.Identity, scale=scale1[:, k, vec(t):vec(t) + 1],
                                                    bias=mod[:, k, vec(t):vec(t) + 1])
                    last.then_inc(h_hi_ready.sem, 1)

                for t in range(TILES):
                    act.wait_ge(*tile_loaded[t].at(l, 1))
                    last = nc.scalar.activation(mix_flat[:, t * D:(t + 1) * D], x_all[:, t, :], ACT.Square,
                                               accum_out=ssq[:, t:t + 1])
                last.then_inc(ssq_ready.sem, 1)
                if l == 0:
                    act.wait_ge(*lam_summed.at(0, 1))
                    nc.scalar.activation(lam_e[:], lam_e[:], ACT.Exp).then_inc(lam_exped.sem, 1)
                for t in range(TILES):
                    h_hi(t)

                for n in range(4 * BLK):
                    i, b = n // BLK, n % BLK
                    lat, con = ps[:, 2 * (n % 3), :], ps[:, 2 * (n % 3) + 1, 0:N_CTX]
                    if b == BLK - 1:
                        act.wait_ge(*unit_used.at(l, D_PROJ + i + 1))
                    else:
                        act.wait_ge(*proj_done.at(l, i * (BLK - 1) + b + 1))
                    if i == 0:
                        if b == 0:
                            act.wait_ge(*halo_zero.at(l, 1))
                        nc.scalar.activation(u[:, b, HALO + LAT0:HALO + LAT0 + N_LAT], lat, ACT.Copy)
                        last = nc.scalar.activation(u[:, b, HALO:HALO + N_CTX], con, ACT.Copy)
                    elif i == 1:
                        if b >= 2:
                            act.wait_ge(*glu_ready.at(l, b - 1))
                        nc.scalar.activation(conv_tmp[:, b % 2, LAT0:C_LEN], lat, ACT.Sigmoid)
                        last = nc.scalar.activation(conv_tmp[:, b % 2, 0:N_CTX], con, ACT.Sigmoid)
                    else:
                        dst = k_t if i == 2 else q_t
                        nc.scalar.activation(dst[:, b, N_CTX:N_TOK], lat, ACT.Copy)
                        last = nc.scalar.activation(dst[:, b, 0:N_CTX], con, ACT.Copy)
                    last.then_inc(proj_copied.sem, 1)
                for t in range(TILES):
                    n = 4 * BLK + t
                    if t == TILES - 1:
                        act.wait_ge(*unit_used.at(l, D_MOD2))
                    else:
                        act.wait_ge(*proj_done.at(l, 4 * (BLK - 1) + t + 1))
                    nc.scalar.activation(v_tok[:, t, :], ps[:, 2 * (n % 3), :], ACT.Copy).then_inc(proj_copied.sem, 1)
                act.wait_ge(*proj_copied.at(l, 4 * BLK + 1))
                act.dma_start(new_cache_v[0, l].rearrange("t h d -> t (h d)"), v_tok[:, 0, :])\
                   .then_inc(cache_stored.sem, 16)
                act.wait_ge(*keys_transposed.at(l, 1))
                act.wait_ge(*glu_ready.at(l, CH))
                nc.scalar.activation(key_rows, ps[:, 6, :], ACT.Copy).then_inc(keys_copied.sem, 1)
                act.wait_ge(*keys_copied.at(l, 1))
                act.dma_start(new_cache_k[0, l].rearrange("t h c d -> t (h c d)"), key_rows)\
                   .then_inc(cache_stored.sem, 16)
                act.wait_ge(*cache_stored.at(l, 2))

                for j in range(CH):
                    act.wait_ge(*centred.at(l, j + 1))
                    if j >= 2:
                        act.wait_ge(*square_used.at(l, j - 1))
                    nc.scalar.activation(conv_tmp[:, j % 2, :], acc[:, j, :], ACT.Square).then_inc(squared.sem, 1)
                act.wait_ge(*square_used.at(l, CH))
                act.wait_ge(*rope_ready.at(l, 2))
                nc.scalar.activation(conv_rstd, ps[:, 2:4, :].rearrange("p b n -> p (b n)")[:, 0:C_LEN], ACT.Sqrt,
                                     scale=1.0 / D_CONV, bias=eps[:]).then_inc(conv_std_ready.sem, 1)
                for j in range(CH):
                    act.wait_ge(*conv_normed.at(l, j + 1))
                    for cols, src in ((slice(0, N_CTX), slice(0, N_CTX)), (slice(N_CTX, N_TOK), slice(LAT0, C_LEN))):
                        last = nc.scalar.activation(mix[:, j, cols], acc[:, j, src], ACT.Silu,
                                                    scale=par_cols[:, l, C_LG + j:C_LG + j + 1],
                                                    bias=par_cols[:, l, C_LB + j:C_LB + j + 1])
                last.then_inc(conv_out_ready.sem, 1)
                def exps(s):
                    t, b0, b = s // H, 3 * (s % 2), s % 2
                    act.wait_ge(*neg_m_ready.at(l, s + 1))
                    for m in range(2):
                        if t > 0:
                            nc.scalar.activation(prob[:, b, m, 0:N_LAT], ps[:, b0 + m, :], ACT.Exp,
                                                 bias=neg_m[:, b, m:m + 1], accum_out=row_sum[:, b, 0, m:m + 1])
                        at = N_LAT if t > 0 else 0
                        last = nc.scalar.activation(prob[:, b, m, at:at + P], ps[:, b0 + 2, tokens(m)], ACT.Exp,
                                                    bias=neg_m[:, b, m:m + 1], accum_out=row_sum[:, b, 1, m:m + 1])
                    last.then_inc(probs_ready.sem, 1)

                def mix_o(t):
                    act.wait_ge(*o_transposed.at(l, t + 1))
                    nc.scalar.activation(mix[:, CH:KD, tokens(t)], ps[:, 6, :].rearrange("p (h n) -> p h n", h=H),
                                         ACT.Copy, scale=sub_cols[:, l:l + 1]).then_inc(o_mixed.sem, 1)

                exps(0)
                exps(1)
                for s in range(ATT):
                    t, h = s // H, s % H
                    act.wait_ge(*a_transposed.at(l, s + 1))
                    if s > 0:
                        act.wait_ge(*pv_done.at(l, s))
                    if t > 0:
                        nc.scalar.activation(a_col[:, 0:N_LAT], ps[:, 6, :], ACT.Copy)
                        last = nc.scalar.activation(a_col[:, N_LAT:N_TOK], ps[:, 7, 0:P], ACT.Copy)
                    else:
                        last = nc.scalar.activation(a_col[:, 0:P], ps[:, 6, 0:P], ACT.Copy)
                    last.then_inc(a_col_ready.sem, 1)
                    if s + 2 < ATT:
                        exps(s + 2)
                    if t > 0 and h == 1:
                        mix_o(t - 1)
                act.wait_ge(*gates_transposed.at(l, 1))
                for v in range(2):
                    for n in range(2):
                        last = nc.scalar.activation(gate1[:, v, n * BANK:(n + 1) * BANK], ps[:, 2 + 2 * v + n, :],
                                                    ACT.Copy)
                last.then_inc(gates_ready.sem, 1)
                mix_o(TILES - 1)
                act.wait_ge(*gates_transposed.at(l, 2))
                for n in range(2):
                    last = nc.scalar.activation(gate2[:, n * BANK:(n + 1) * BANK], ps[0:CAP, 4 + n, :], ACT.Copy)
                last.then_inc(gates_ready.sem, 1)

                def unit_rows(i):
                    act.wait_ge(*x2_ready.at(l, i + 1))
                    if i > 0:
                        act.wait_ge(*unit_stored.at(l, i))
                        act.wait_ge(*x2_transposed.at(l, i))
                    nc.scalar.activation(x_norm[:], x_tile[:, i % 2, :], ACT.Square,
                                         accum_out=ssq[:, TILES:TILES + 1]).then_inc(ssq2_ready.sem, 1)
                    act.wait_ge(*rstd2_ready.at(l, i + 1))
                    nc.scalar.activation(x_norm[:], x_tile[:, i % 2, :], ACT.Copy, scale=rstd[:, TILES:TILES + 1])\
                      .then_inc(unit_row_ready.sem, 1)
                    act.wait_ge(*unit_row_ready.at(l, i + 1))
                    act.dma_start(x_unit[tokens(OUT_TILES[i]), :], x_norm[:]).then_inc(unit_stored.sem, 16)

                def h2_hi(i):
                    v = vec(OUT_TILES[i])
                    act.wait_ge(*x2_transposed.at(l, i + 1))
                    if i > 0:
                        act.wait_ge(*logits_done.at(l, i))
                    for k in range(4, KD):
                        last = nc.scalar.activation(h2_t[:, k, :], ps[:, 5, tokens(k - 4)], ACT.Identity,
                                                    scale=scale2[:, k, v:v + 1], bias=mod[:, 3 * KD + k, v:v + 1])
                    last.then_inc(h2_hi_ready.sem, 1)

                def router_exp(i):
                    act.wait_ge(*r_max_ready.at(l, i + 1))
                    nc.scalar.activation(r_exp[:], ps[:, 6, 0:EXPERTS], ACT.Exp, bias=r_max[:],
                                         accum_out=r_sum[:]).then_inc(r_exp_ready.sem, 1)

                unit_rows(0)
                h2_hi(0)
                for i in range(1, TILES - 1):
                    unit_rows(i)
                    router_exp(i - 1)
                    h2_hi(i)
                router_exp(TILES - 2)
                unit_rows(TILES - 1)
                h2_hi(TILES - 1)
                router_exp(TILES - 1)

                with act.Fori(0, EXPERTS) as e:
                    for half in range(2):
                        act.wait_ge(*unit_used.at(l, e * 6 + (DENSE_UNITS + 2 * half + 1)))
                        nc.scalar.activation(silu_g[:, half, :].rearrange("p (f n) -> p f n", f=BLK),
                                             halves(2 * half), ACT.Silu)\
                          .then_inc(silu_ready.sem, 1)

            for t in range(TILES):
                act.wait_ge(*tile_loaded[t].at(DEPTH, 1))
                last = nc.scalar.activation(mix_flat[:, t * D:(t + 1) * D], x_all[:, t, :], ACT.Square,
                                               accum_out=ssq[:, t:t + 1])
            last.then_inc(ssq_ready.sem, 1)
            for t in range(TILES):
                act.wait_ge(*y_ready.at(0, t + 1))
                dst = y_prompt[0] if t == 0 else y_sample[0, (t - 1) * P:t * P, :]
                act.dma_start(dst, x_all[:, t, :]).then_inc(y_stored.sem, 16)
            act.wait_ge(*y_stored.at(0, TILES))
            act.wait_ge(*cache_stored.at(DEPTH - 1, 2))

        @block.vector
        def _(dve):
            steps = [0]

            def step(ins):
                ins.then_inc(dve_step.sem, 1)
                steps[0] += 1
                return steps[0]

            def own(n):
                dve.wait_ge(dve_step.sem, n)

            def setup():
                dve.wait_ge(*misc_loaded.at(0, 4 * DEPTH + 3 * DEPTH + 2))
                own(step(nc.vector.tensor_tensor(lam_prod, lam_rows[:, :, 0:4:2, :], lam_rows[:, :, 1:4:2, :], ALU.mult)))
                nc.vector.tensor_reduce(lam_e[:], lam_prod, AX, ALU.add).then_inc(lam_summed.sem, 1)
                dve.wait_ge(*setup_transposed.at(0, 3))
                nc.vector.tensor_copy(conv_cols[:].rearrange("p l n -> p (l n)"), ps[:, 1, 0:DEPTH * TAPS * CH])
                nc.vector.tensor_copy(par_cols[:].rearrange("p l n -> p (l n)"),
                                      ps[:, 1, DEPTH * TAPS * CH:DEPTH * (TAPS * CH + C_ALL)])
                own(step(nc.vector.tensor_copy(past_k_t[:].rearrange("p l h n -> p l (h n)"), ps[:, 2:2 + DEPTH, :])))
                dve.wait_ge(*lam_exped.at(0, 1))
                for l in range(DEPTH):
                    nc.vector.tensor_scalar(neg_lam[:, l:l + 1], lam_e[:, l, 1:2], lam_e[:, l, 0:1], -lam_init[l],
                                            ALU.subtract, ALU.add)
                    last = nc.vector.tensor_scalar(sub_cols[:, l:l + 1], par_cols[:, l, C_SUB:C_SUB + 1],
                                                   1.0 - lam_init[l], None, ALU.mult)
                own(step(last))
                own(step(nc.vector.memset(map_scale[:], 0.0)))
                for m in range(2):
                    last = nc.vector.memset(map_scale[m * HD:(m + 1) * HD, m:m + 1], HD ** -0.5)
                last.then_inc(setup_copied.sem, 1)

            for l in range(DEPTH):
                def take_mod(bank, at, units):
                    lo, n = units[0] * BLK, len(units) * BLK
                    bias = par_cols[:, l, C_BMOD + lo:C_BMOD + lo + n].unsqueeze(2).to_broadcast([P, n, 2])
                    src = ps[:, bank, 2 * at * BLK:2 * (at * BLK + n)].rearrange("p (n v) -> p n v", v=2)
                    return nc.vector.tensor_tensor(mod[:, lo:lo + n, :], src, bias, ALU.add)

                def gain(dst, q, at):
                    g = par_cols[:, l, at:at + KD].unsqueeze(2).to_broadcast([P, KD, 2])
                    return nc.vector.scalar_tensor_tensor(dst[:], mod[:, q * KD:(q + 1) * KD, :], 1.0, g,
                                                          ALU.add, ALU.mult)

                dve.wait_ge(*ssq_ready.at(l, 1))
                nc.vector.tensor_scalar(mean_sq[:, 0:TILES], ssq[:, 0:TILES], 1.0 / D, EPS,
                                        ALU.mult, ALU.add).then_inc(mean_sq_ready.sem, 1)
                dve.wait_ge(*rstd_ready.at(l, 1))
                for t in range(TILES):
                    nc.vector.tensor_scalar(x_all[:, t, :], x_all[:, t, :], rstd[:, t:t + 1], None, ALU.mult)\
                      .then_inc(x_norm_ready.sem, 1)
                if l == 0:
                    setup()
                dve.wait_ge(*unit_used.at(l, MOD_FIRST))
                own(step(take_mod(7, 0, MOD_ORDER[:MOD_FIRST])))
                gain(scale1, 1, C_N1).then_inc(mod1_ready.sem, 1)
                dve.wait_ge(*mod1_ready.at(l, 1))
                for t in range(TILES):
                    dve.wait_ge(*x_transposed.at(l, t + 1))
                    v = vec(t)
                    for k in range(4):
                        last = nc.vector.tensor_scalar(mix[:, k, tokens(t)], ps[:, 2 * (t % 3), tokens(k)],
                                                       scale1[:, k, v:v + 1], mod[:, k, v:v + 1],
                                                       ALU.mult, ALU.add)
                    last.then_inc(h_lo_ready.sem, 1)

                for b in range(CH):
                    dve.wait_ge(*proj_copied.at(l, BLK + b + 1))
                    for ucol, col, n in ((HALO, 0, N_CTX), (HALO + LAT0, LAT0, N_LAT)):
                        dst = u[:, b, ucol:ucol + n]
                        last = nc.vector.tensor_tensor(dst, dst, conv_tmp[:, b % 2, col:col + n], ALU.mult)
                    last.then_inc(glu_ready.sem, 1)
                dve.wait_ge(*glu_ready.at(l, CH))

                done = [0] * CH

                def taps(t0, t1):
                    for t in range(t0, t1):
                        for j in range(CH):
                            w = conv_cols[:, l, t * CH + j:t * CH + j + 1]
                            src = u[:, j, t:t + C_LEN]
                            if t == 0:
                                ins = nc.vector.tensor_scalar(acc[:, j, :], src, w,
                                                              par_cols[:, l, C_CB + j:C_CB + j + 1],
                                                              ALU.mult, ALU.add)
                            else:
                                own(done[j])
                                ins = nc.vector.scalar_tensor_tensor(acc[:, j, :], src, w, acc[:, j, :],
                                                                     ALU.mult, ALU.add)
                            if t == TAPS - 1:
                                ins.then_inc(conv_ready.sem, 1)
                            else:
                                done[j] = step(ins)

                def swaps(i):
                    for h in range(H):
                        dve.wait_ge(*proj_copied.at(l, (2 + i) * BLK + h + 1))
                        src = (k_t, q_t)[i][:, h, N_CTX:N_TOK]
                        nc.vector.stream_shuffle(rope_tmp[:, i * H + h, :], src, [p ^ 16 for p in range(32)])\
                          .then_inc(rope_shuffled.sem, 1)

                taps(0, TAPS // 2)
                swaps(0)
                taps(TAPS // 2, TAPS)
                swaps(1)

                dve.wait_ge(*unit_used.at(l, D_MOD2 + 4))
                take_mod(7, 0, MOD_ORDER[4:6])
                own(step(take_mod(7, 2, MOD_ORDER[6:8])))

                dve.wait_ge(*mean_ready.at(l, 1))
                mean = ps[:, 0:2, :].rearrange("p b n -> p (b n)")[:, 0:C_LEN]
                for j in range(CH):
                    nc.vector.scalar_tensor_tensor(acc[:, j, :], mean, -1.0 / D_CONV, acc[:, j, :],
                                                   ALU.mult, ALU.add).then_inc(centred.sem, 1)
                dve.wait_ge(*conv_std_ready.at(l, 1))
                own(step(nc.vector.reciprocal(conv_rstd, conv_rstd)))
                for j in range(CH):
                    nc.vector.tensor_tensor(acc[:, j, :], acc[:, j, :], conv_rstd, ALU.mult)\
                      .then_inc(conv_normed.sem, 1)
                dve.wait_ge(*unit_used.at(l, D_OUT))
                own(step(take_mod(6, 0, MOD_ORDER[8:12])))
                own(step(gain(scale2, 4, C_N2)))
                for dst, q, src in ((shift2_x, 3, mod), (scale2_x, 0, scale2)):
                    cols = src[:, q * KD:(q + 1) * KD, :]
                    nc.vector.tensor_copy(dst[:, :, 0:CAP_LAT], cols[:, :, 1:2].to_broadcast([P, KD, CAP_LAT]))
                    last = nc.vector.tensor_copy(dst[:, :, CAP_LAT:CAP],
                                                 cols[:, :, 0:1].to_broadcast([P, KD, CAP_CTX]))
                last.then_inc(mod2_ready.sem, 1)
                def spread_gates():
                    dve.wait_ge(*conv_out_ready.at(l, 1))
                    for v in range(2):
                        nc.vector.tensor_copy(gate1_cols[:, v],
                                              mod[:, 2 * KD:3 * KD, v:v + 1].to_broadcast([P, KD, P]))
                    g2 = mod[:, 5 * KD:6 * KD, :]
                    nc.vector.tensor_copy(gate2_cols[:, :, 0:CAP_LAT], g2[:, :, 1:2].to_broadcast([P, KD, CAP_LAT]))
                    nc.vector.tensor_copy(gate2_cols[:, :, CAP_LAT:CAP],
                                          g2[:, :, 0:1].to_broadcast([P, KD, CAP_CTX]))\
                      .then_inc(gate_cols_ready.sem, 1)

                def row_max(s):
                    t, b0, b = s // H, 3 * (s % 2), s % 2
                    dve.wait_ge(*scores_done.at(l, s + 1))
                    tail = ps[:, b0 + 2, 0:2 * P].rearrange("p (m n) -> p m n", m=2)
                    if t > 0:
                        nc.vector.tensor_reduce(neg_max[:, b, 0, :], ps[:, b0:b0 + 2, :], AX, ALU.max, negate=True)
                        own(step(nc.vector.tensor_reduce(neg_max[:, b, 1, :], tail, AX, ALU.max, negate=True)))
                        nc.vector.tensor_tensor(neg_m[:, b, :], neg_max[:, b, 0, :], neg_max[:, b, 1, :], ALU.min)\
                          .then_inc(neg_m_ready.sem, 1)
                    else:
                        nc.vector.tensor_reduce(neg_m[:, b, :], tail, AX, ALU.max, negate=True)\
                          .then_inc(neg_m_ready.sem, 1)

                def o_norm(t):
                    b = t % 2
                    own(step(nc.vector.tensor_tensor(o_sq[:], o_tok[:, b], o_tok[:, b], ALU.mult)))
                    own(step(nc.vector.tensor_reduce(o_ss[:, b, :], o_sq[:], AX, ALU.add)))
                    nc.vector.tensor_scalar(o_ss[:, b, :], o_ss[:, b, :], 1.0 / VD, EPS, ALU.mult, ALU.add)\
                      .then_inc(o_mean_sq_ready.sem, 1)

                def o_scale(t):
                    b = t % 2
                    dve.wait_ge(*o_rstd_ready.at(l, t + 1))
                    nc.vector.tensor_tensor(o_tok[:, b], o_tok[:, b],
                                            o_rstd[:, b, :].unsqueeze(2).to_broadcast([P, H, VD]), ALU.mult)\
                      .then_inc(o_normed.sem, 1)

                def take_o(s):
                    dve.wait_ge(*pv_done.at(l, s + 1))
                    nc.vector.tensor_scalar(o_tok[:, (s // H) % 2, s % H, :], ps[:, 7, 2 * P:3 * P],
                                            row_r[:, s % 2, 0:1], None, ALU.mult)\
                      .then_inc(o_copied.sem, 1)
                    if s % H == H - 1:
                        dve.wait_ge(*o_copied.at(l, s + 1))
                        o_norm(s // H)

                row_max(0)
                row_max(1)
                spread_gates()
                for s in range(ATT):
                    t, b = s // H, s % 2
                    n = N_TOK if t > 0 else N_CTX
                    total = row_sum[:, b, 1, :]
                    dve.wait_ge(*probs_ready.at(l, s + 1))
                    if t > 0:
                        own(step(nc.vector.tensor_tensor(total, row_sum[:, b, 0, :], total, ALU.add)))
                    own(step(nc.vector.reciprocal(row_r[:, b, :], total)))
                    own(step(nc.vector.scalar_tensor_tensor(row_c[:, b:b + 1], total[:, 0:1], neg_lam[:, l:l + 1],
                                                            row_r[:, b, 1:2], ALU.mult, ALU.mult)))
                    nc.vector.scalar_tensor_tensor(a_row[:, b, 0:n], prob[:, b, 1, 0:n], row_c[:, b:b + 1],
                                                   prob[:, b, 0, 0:n], ALU.mult, ALU.add)\
                      .then_inc(a_ready.sem, 1)
                    if s > H and s % H == 1:
                        o_scale(s // H - 1)
                    if s > 0:
                        take_o(s - 1)
                    if s + 2 < ATT:
                        row_max(s + 2)
                take_o(ATT - 1)
                o_scale(TILES - 1)

                out_tmp = conv_tmp[:, :, :].rearrange("p b n -> p (b n)")[:, 0:D]

                def x2(i):
                    if i == TILES - 1:
                        dve.wait_ge(*unit_used.at(l, DENSE_UNITS))
                    else:
                        dve.wait_ge(*out_done.at(l, i + 1))
                    if i == 0:
                        dve.wait_ge(*gates_ready.at(l, 1))
                    b = i % 2
                    y = ps[:, 2 * b:2 * b + 2, :].rearrange("p b n -> p (b n)")
                    own(step(nc.vector.tensor_tensor(out_tmp, y, gate1[:, vec(OUT_TILES[i]), :], ALU.mult)))
                    dve.wait_ge(*x_loaded[b].at(l, i // 2 + 1))
                    nc.vector.tensor_tensor(x_tile[:, b, :], x_tile[:, b, :], out_tmp, ALU.add)\
                      .then_inc(x2_ready.sem, 1)

                def mean_square(i):
                    dve.wait_ge(*ssq2_ready.at(l, i + 1))
                    nc.vector.tensor_scalar(mean_sq[:, TILES:TILES + 1], ssq[:, TILES:TILES + 1], 1.0 / D, EPS,
                                            ALU.mult, ALU.add).then_inc(mean_sq2_ready.sem, 1)

                def h2_lo(i):
                    dve.wait_ge(*x2_transposed.at(l, i + 1))
                    if i > 0:
                        dve.wait_ge(*logits_done.at(l, i))
                    v = vec(OUT_TILES[i])
                    for k in range(4):
                        last = nc.vector.tensor_scalar(h2_t[:, k, :], ps[:, 4, tokens(k)], scale2[:, k, v:v + 1],
                                                       mod[:, 3 * KD + k, v:v + 1], ALU.mult, ALU.add)
                    last.then_inc(h2_lo_ready.sem, 1)

                def router_max(i):
                    dve.wait_ge(*logits_done.at(l, i + 1))
                    nc.vector.tensor_reduce(r_max[:], ps[:, 6, 0:EXPERTS], AX, ALU.max, negate=True)\
                      .then_inc(r_max_ready.sem, 1)

                def affinity(i):
                    dve.wait_ge(*r_exp_ready.at(l, i + 1))
                    own(step(nc.vector.reciprocal(r_sum[:], r_sum[:])))
                    nc.vector.tensor_scalar(aff[:], r_exp[:], r_sum[:], None, ALU.mult).then_inc(aff_ready.sem, 1)

                def take_aff(i):
                    dve.wait_ge(*aff_transposed.at(l, i + 1))
                    nc.vector.tensor_copy(aff_t[:, tokens(OUT_TILES[i])], ps[0:EXPERTS, 7, 0:P])\
                      .then_inc(aff_copied.sem, 1)
                    dve.wait_ge(*aff_copied.at(l, i + 1))

                def top_rounds(cols, at, rounds):
                    left = aff_t[:, cols]
                    for r in rounds:
                        i = at + 8 * r
                        own(step(nc.vector.max(top_v[:, i:i + 8], left)))
                        nc.vector.max_index(top_i[:, i:i + 8], top_v[:, i:i + 8], left)
                        own(step(nc.vector.match_replace(left, top_v[:, i:i + 8], left, -1.0)))

                def top_latent(r0, r1):
                    top_rounds(slice(N_CTX, N_TOK), 0, range(r0, r1))

                last = TILES - 1
                x2(0)
                mean_square(0)
                x2(1)
                for i in range(last):
                    h2_lo(i)
                    if i + 1 < last:
                        mean_square(i + 1)
                    if i + 2 < last:
                        x2(i + 2)
                    if i > 0:
                        take_aff(i - 1)
                    router_max(i)
                    affinity(i)
                take_aff(last - 1)
                x2(last)
                top_latent(0, 1)
                mean_square(last)
                top_latent(1, 4)
                h2_lo(last)
                top_latent(4, 5)
                router_max(last)
                top_latent(5, 6)
                affinity(last)
                top_latent(6, 7)
                take_aff(last)
                top_latent(7, CAP_LAT // 8)
                top_rounds(slice(0, N_CTX), CAP_LAT, range(CAP_CTX // 8))
                own(step(nc.vector.tensor_copy(top_f, top_i)))
                nc.vector.tensor_scalar_add(top_f[:, 0:CAP_LAT], top_f[:, 0:CAP_LAT], float(N_CTX))\
                  .then_inc(top_ready.sem, 1)
                dve.wait_ge(*top_transposed.at(l, 1))
                nc.vector.tensor_copy(row_idx[:], ps[0:CAP, 4, 0:EXPERTS])
                nc.vector.tensor_copy(gsel[:], ps[0:CAP, 5, 0:EXPERTS]).then_inc(result_taken.sem, 1)
                dve.wait_ge(*result_taken.at(l, 1))

                def modulate_picked(e, b):
                    dve.wait_ge(*picked_transposed.at(l, e + 1))
                    dst = picked_t[:, b, :, 0:CAP].rearrange("p (a k) n -> p a k n", a=2)
                    src = ps[:, 6:8, 0:4 * CAP].rearrange("p a (k n) -> p a k n", k=4)
                    sc = scale2_x[:].rearrange("p (a k) n -> p a k n", a=2)
                    sh = shift2_x[:].rearrange("p (a k) n -> p a k n", a=2)
                    nc.vector.tensor_tensor(dst, src, sc, ALU.mult).then_inc(picked_scaled.sem, 1)
                    dve.wait_ge(*picked_scaled.at(l, e + 1))
                    nc.vector.tensor_tensor(dst, dst, sh, ALU.add).then_inc(picked_ready.sem, 1)

                def gated_hidden(e):
                    for half in range(2):
                        dve.wait_ge(*unit_used.at(l, e * 6 + (DENSE_UNITS + 2 * half + 2)))
                        dve.wait_ge(*silu_ready.at(l, e * 2 + half + 1))
                        nc.vector.tensor_tensor(hid[:, half * BLK:(half + 1) * BLK, :],
                                                silu_g[:, half, :].rearrange("p (f n) -> p f n", f=BLK),
                                                halves(2 * half + 1), ALU.mult).then_inc(hid_ready.sem, 1)

                def gated_result(e, b, rnd):
                    dve.wait_ge(*unit_used.at(l, e * 6 + (DENSE_UNITS + 6)))
                    dve.wait_ge(*residual_written[b].at(l, rnd + (3 - b)))
                    nc.vector.scalar_tensor_tensor(added[:, b, :], ps[0:CAP, 4:6, :].rearrange("p b n -> p (b n)"),
                                                   gsel[:, bass.ds(e, 1)], gate2[:], ALU.mult, ALU.mult)\
                      .then_inc(result_taken.sem, 1)

                with dve.Fori(0, EXPERTS // 2) as r:
                    modulate_picked(r * 2, 0)
                    gated_hidden(r * 2)
                    modulate_picked(r * 2 + 1, 1)
                    gated_result(r * 2, 0, r)
                    gated_hidden(r * 2 + 1)
                    gated_result(r * 2 + 1, 1, r)

            gain_rows = h2_t.rearrange("p k n -> p (k n)")
            dve.wait_ge(*ssq_ready.at(DEPTH, 1))
            nc.vector.tensor_scalar(mean_sq[:, 0:TILES], ssq[:, 0:TILES], 1.0 / D, EPS, ALU.mult, ALU.add)\
              .then_inc(mean_sq_ready.sem, 1)
            dve.wait_ge(*gain_loaded.at(0, 1))
            dve.wait_ge(*rstd_ready.at(DEPTH, 1))
            for t in range(TILES):
                nc.vector.scalar_tensor_tensor(x_all[:, t, :], x_all[:, t, :], rstd[:, t:t + 1], gain_rows,
                                               ALU.mult, ALU.mult).then_inc(y_ready.sem, 1)

        @block.gpsimd
        def _(pool):
            steps = [0]

            def step(ins):
                ins.then_inc(pool_step.sem, 1)
                steps[0] += 1
                return steps[0]

            def own(n):
                pool.wait_ge(pool_step.sem, n)

            def inv_sqrt(dst, src, ready):
                nc.gpsimd.tensor_tensor(dst, src, neg_half[:, 0:src.shape[1]], ALU.pow).then_inc(ready.sem, 1)

            nc.gpsimd.memset(eps[:], EPS)
            nc.gpsimd.memset(neg_half[:], -0.5)
            own(step(nc.gpsimd.memset(ident[:], 0.0)))
            nc.gpsimd.affine_select(out=ident[:], in_=ident[:], compare_op=ALU.not_equal, fill=1.0, base=0,
                                    pattern=[[-1, P]], channel_multiplier=1).then_inc(consts_ready.sem, 1)
            nc.gpsimd.memset(ones[:], 1.0).then_inc(consts_ready.sem, 1)

            def load_x(dst, l, t, loaded):
                src = input_rows(t) if l == 0 else x_res[tokens(t), :]
                pool.dma_start(dst, src).then_inc(loaded.sem, 16)

            for l in range(DEPTH):
                for t in range(TILES):
                    load_x(x_all[:, t, :], l, t, tile_loaded[t])
                for i in range(2):
                    load_x(x_tile[:, i, :], l, OUT_TILES[i], x_loaded[i])
                pool.wait_ge(*mean_sq_ready.at(l, 1))
                inv_sqrt(rstd[:, 0:TILES], mean_sq[:, 0:TILES], rstd_ready)
                for at in (0, HALO + N_CTX, U_LEN - HALO):
                    last = nc.gpsimd.memset(u[:, :, at:at + HALO], 0.0)
                last.then_inc(halo_zero.sem, 1)
                def rotate(i):
                    for h in range(H):
                        x = (k_t, q_t)[i][:, h, N_CTX:N_TOK]
                        sw = rope_tmp[:, i * H + h, :]
                        pool.wait_ge(*rope_shuffled.at(l, i * H + h + 1))
                        nc.gpsimd.tensor_tensor(sw, sw, sin_sb[:], ALU.mult)
                        own(step(nc.gpsimd.tensor_tensor(x, x, cos_sb[:], ALU.mult)))
                        nc.gpsimd.tensor_tensor(x, x, sw, ALU.add).then_inc(rope_ready.sem, 1)

                if l == 0:
                    pool.wait_ge(*setup_copied.at(0, 1))
                    pool.wait_ge(*misc_loaded.at(0, 4 * DEPTH + 3 * DEPTH + 2))
                rotate(0)
                rotate(1)

                def o_inv_sqrt(t):
                    pool.wait_ge(*o_mean_sq_ready.at(l, t + 1))
                    inv_sqrt(o_rstd[:, t % 2, :], o_ss[:, t % 2, :], o_rstd_ready)

                pool.wait_ge(*rope_ready.at(l, 2 * H))
                for s in range(ATT):
                    t, h, b = s // H, s % H, s % 2
                    if s >= 2:
                        pool.wait_ge(*scores_done.at(l, s - 1))
                    for m in range(2):
                        last = nc.gpsimd.tensor_scalar(q_pad[:, b, m, :], q_t[:, h, tokens(t)],
                                                       map_scale[:, m:m + 1], None, ALU.mult)
                    last.then_inc(q_padded.sem, 1)
                    if s > H and s % H == H - 1:
                        o_inv_sqrt(s // H - 1)
                o_inv_sqrt(TILES - 1)

                pool.wait_ge(*pv_done.at(l, ATT))
                nc.gpsimd.memset(picked_t[:, :, :, CAP:CAP_W], 0.0).then_inc(padding_zero.sem, 1)

                for i in range(TILES):
                    b = i % 2
                    pool.wait_ge(*x2_ready.at(l, i + 1))
                    pool.dma_start(x_res[tokens(OUT_TILES[i]), :], x_tile[:, b, :])\
                        .then_inc(residual_written[b].sem, 16)
                    pool.wait_ge(*mean_sq2_ready.at(l, i + 1))
                    inv_sqrt(rstd[:, TILES:TILES + 1], mean_sq[:, TILES:TILES + 1], rstd2_ready)
                    if i + 2 < TILES:
                        pool.wait_ge(*residual_written[b].at(l, i // 2 + 1))
                        pool.wait_ge(*unit_row_ready.at(l, i + 1))
                        load_x(x_tile[:, b, :], l, OUT_TILES[i + 2], x_loaded[b])

                def gather(e):
                    b = e % 2
                    if e >= 2:
                        pool.wait_ge(*picked_transposed.at(l, e - 1))
                    nc.gpsimd.indirect_dma_start(
                        out=picked[:, b, :], out_offset=None, in_=x_unit,
                        in_offset=bass.IndirectOffsetOnAxis(ap=row_idx[:, e:e + 1], axis=0))\
                      .then_inc(gathered[b].sem, 16)

                pool.wait_ge(*result_taken.at(l, 1))
                pool.wait_ge(*unit_stored.at(l, TILES))
                gather(0)
                gather(1)
                if l == DEPTH - 1:
                    pool.dma_start(h2_t.rearrange("p k n -> p (k n)"),
                                   final_norm_g.rearrange("(a n) -> a n", a=1).to_broadcast([P, D]))\
                        .then_inc(gain_loaded.sem, 16)
                pool.wait_ge(*residual_written[0].at(l, 3))
                pool.wait_ge(*residual_written[1].at(l, 2))
                for e in range(EXPERTS):
                    b = e % 2
                    if e > 0:
                        pool.wait_ge(*residual_written[1 - b].at(l, 2 + b + (e + 1) // 2))
                    pool.wait_ge(*result_taken.at(l, e + 2))
                    nc.gpsimd.indirect_dma_start(
                        out=x_res, out_offset=bass.IndirectOffsetOnAxis(ap=row_idx[:, e:e + 1], axis=0),
                        in_=added[:, b, :], in_offset=None, compute_op=ALU.add)\
                      .then_inc(residual_written[b].sem, 16)
                    if e + 2 < EXPERTS:
                        gather(e + 2)
                pool.wait_ge(*residual_written[1].at(l, 2 + EXPERTS // 2))
                pool.wait_ge(*residual_written[0].at(l, 3 + EXPERTS // 2))

            for t in range(TILES):
                load_x(x_all[:, t, :], DEPTH, t, tile_loaded[t])
            pool.wait_ge(*mean_sq_ready.at(DEPTH, 1))
            inv_sqrt(rstd[:, 0:TILES], mean_sq[:, 0:TILES], rstd_ready)


_INS = ['x_prompt', 'x_sample', 'c', 'cache_k', 'cache_v', 'c_ctx', 'norm1_g', 'w_mod', 'b_mod', 'w_in', 'conv_w',
        'conv_b', 'conv_ln_g', 'conv_ln_b', 'lambda_q1', 'lambda_k1', 'lambda_q2', 'lambda_k2', 'subln_g', 'w_out',
        'norm2_g', 'w_router', 'w_gate', 'w_up', 'w_down', 'final_norm_g']
_OUTS = [((1, N_CTX, D), 'float32'), ((1, N_LAT, D), 'float32'), ((1, DEPTH, N_CTX, H, 2, HD), 'float32'),
         ((1, DEPTH, N_CTX, H, VD), 'float32')]


def rope_constants():
    t = np.arange(N_LAT)
    inv = np.float32(ROPE_BASE) ** (-np.arange(0, ROPE_AXIS, 2, dtype=np.float32) / np.float32(ROPE_AXIS))
    p = np.arange(P)
    pos = np.where((p[:, None] % HD) < ROPE_AXIS, (t // GRID_W)[None, :], (t % GRID_W)[None, :]).astype(np.float32)
    angle = pos * inv[p % (ROPE_AXIS // 2)][:, None].astype(np.float32)
    sign = np.where(p % ROPE_AXIS < ROPE_AXIS // 2, -1.0, 1.0).astype(np.float32)
    return np.cos(angle).astype(np.float32), (np.sin(angle) * sign[:, None]).astype(np.float32)


def kernel(**inputs):
    import numpy as _np
    import concourse.bacc as _bacc
    from concourse import mybir as _mybir
    from concourse.bass_utils import run_bass_kernel_spmd as _run

    nc = _bacc.Bacc("TRN2", target_bir_lowering=False, num_devices=1)
    given = {name: _np.ascontiguousarray(inputs[name]) for name in _INS}
    given["rope_cos"], given["rope_sin"] = rope_constants()
    arrays, args = {}, []
    for name, a in given.items():
        arrays[f"in_{name}_dram"] = a
        args.append(nc.dram_tensor(f"in_{name}_dram", a.shape, _mybir.dt.from_np(a.dtype), kind="ExternalInput").ap())
    for i, (shape, dtype) in enumerate(_OUTS):
        dt = _mybir.dt.from_np(_np.dtype(dtype))
        args.append(nc.dram_tensor(f"out_{i}_dram", shape, dt, kind="ExternalOutput").ap())
    build(nc, *args)
    r = _run(nc, [arrays], core_ids=[0])
    return tuple(r.results[0][f"out_{i}_dram"] for i in range(len(_OUTS)))
```
